# Optimizing a Trainium2 kernel written in Bass

```python
import jax, jax.numpy as jnp
from jax import lax
import numpy as np

D_MODEL = 2048
BATCH = 1
SEQ = 256
DEPTH = 1

GRID_W = 64
MIX_WIDTH = D_MODEL
CONV_WIDTH = MIX_WIDTH // 2
NA_HEADS = 16
NA_HEAD_DIM = (MIX_WIDTH - CONV_WIDTH) // NA_HEADS
NA_WIDTH = NA_HEADS * NA_HEAD_DIM
CONV_KERNEL = 31
WIN_ROWS_MAX = 8
WIN_COLS = 16
D_FF = 4 * D_MODEL
IN_COLS = 2 * CONV_WIDTH + 3 * NA_WIDTH
RMS_EPS = 1e-6
LN_EPS = 1e-5
NEG_INF = -1e30


def rms_norm(x, g):
    xf = x.astype(jnp.float32)
    y = xf * lax.rsqrt(jnp.mean(xf * xf, axis=-1, keepdims=True) + RMS_EPS)
    return (y * g.astype(jnp.float32)).astype(x.dtype)

def layer_norm(x, g, b):
    xf = x.astype(jnp.float32)
    mu = jnp.mean(xf, axis=-1, keepdims=True)
    xc = xf - mu
    var = jnp.mean(xc * xc, axis=-1, keepdims=True)
    y = xc * lax.rsqrt(var + LN_EPS) * g.astype(jnp.float32) + b.astype(jnp.float32)
    return y.astype(x.dtype)

def conformer_conv_group(a, gate, w_dw, b_dw, ln_g, ln_b):
    u = a * jax.nn.sigmoid(gate)
    u = lax.conv_general_dilated(
        u, w_dw[:, None, :].astype(u.dtype),
        window_strides=(1,),
        padding=[(CONV_KERNEL // 2, CONV_KERNEL // 2)],
        dimension_numbers=("NWC", "WIO", "NWC"),
        feature_group_count=CONV_WIDTH,
    ) + b_dw.astype(u.dtype)
    return jax.nn.silu(layer_norm(u, ln_g, ln_b))

def neighbourhood_attention_group(q, k, v, rpb):
    B, T, _ = q.shape
    rows = T // GRID_W
    kr = min(WIN_ROWS_MAX, rows)
    r = np.arange(rows)
    c = np.arange(GRID_W)
    row_start = np.clip(r - kr // 2, 0, rows - kr)
    row_idx = row_start[:, None] + np.arange(kr)[None, :]
    col_start = np.clip(c - WIN_COLS // 2, 0, GRID_W - WIN_COLS)
    col_mask = (c[None, :] >= col_start[:, None]) & (c[None, :] < col_start[:, None] + WIN_COLS)
    dr = row_idx - r[:, None] + (WIN_ROWS_MAX - 1)
    dc = np.clip(c[None, :] - c[:, None], -(WIN_COLS - 1), WIN_COLS - 1) + (WIN_COLS - 1)
    bias = rpb[:, dr[:, None, :, None], dc[None, :, None, :]].astype(jnp.float32)

    def to_grid(t):
        return t.reshape(B, rows, GRID_W, NA_HEADS, NA_HEAD_DIM)

    qg, kg, vg = to_grid(q), to_grid(k), to_grid(v)
    k_rows = kg[:, row_idx]
    v_rows = vg[:, row_idx]
    s = jnp.einsum("brwhd,brkvhd->bhrwkv", qg, k_rows,
                   preferred_element_type=jnp.float32) * (NA_HEAD_DIM ** -0.5)
    s = jnp.where(col_mask[:, None, :], s + bias, NEG_INF)
    p = jax.nn.softmax(s.reshape(B, NA_HEADS, rows, GRID_W, kr * GRID_W), axis=-1)
    p = p.reshape(s.shape).astype(v.dtype)
    o = jnp.einsum("bhrwkv,brkvhd->brwhd", p, v_rows)
    return o.reshape(B, T, NA_WIDTH)

def first_inputs(seed: int = 0) -> dict:
    key = jax.random.key(seed)
    ks = jax.random.split(key, 16)
    f32 = jnp.float32
    x = jax.random.normal(ks[0], (BATCH, SEQ, D_MODEL), f32)
    w_in = jax.random.normal(ks[1], (DEPTH, D_MODEL, IN_COLS), f32) * D_MODEL ** -0.5
    w_dw = jax.random.normal(ks[2], (DEPTH, CONV_KERNEL, CONV_WIDTH), f32) * CONV_KERNEL ** -0.5
    b_dw = jax.random.normal(ks[3], (DEPTH, CONV_WIDTH), f32) * 0.01
    conv_ln_g = 1.0 + 0.05 * jax.random.normal(ks[4], (DEPTH, CONV_WIDTH), f32)
    conv_ln_b = 0.01 * jax.random.normal(ks[5], (DEPTH, CONV_WIDTH), f32)
    rpb = 0.02 * jax.random.normal(ks[6], (DEPTH, NA_HEADS, 2 * WIN_ROWS_MAX - 1, 2 * WIN_COLS - 1), f32)
    w_out = jax.random.normal(ks[7], (DEPTH, MIX_WIDTH, D_MODEL), f32) * MIX_WIDTH ** -0.5
    w_up = jax.random.normal(ks[8], (DEPTH, D_MODEL, D_FF), f32) * D_MODEL ** -0.5
    w_down = jax.random.normal(ks[9], (DEPTH, D_FF, D_MODEL), f32) * D_FF ** -0.5
    pre_mix_g = 1.0 + 0.05 * jax.random.normal(ks[10], (DEPTH, D_MODEL), f32)
    post_mix_g = 1.0 + 0.05 * jax.random.normal(ks[11], (DEPTH, D_MODEL), f32)
    pre_mlp_g = 1.0 + 0.05 * jax.random.normal(ks[12], (DEPTH, D_MODEL), f32)
    post_mlp_g = 1.0 + 0.05 * jax.random.normal(ks[13], (DEPTH, D_MODEL), f32)
    return {"x": x, "w_in": w_in, "w_dw": w_dw, "b_dw": b_dw, "conv_ln_g": conv_ln_g,
            "conv_ln_b": conv_ln_b, "rpb": rpb, "w_out": w_out, "w_up": w_up, "w_down": w_down,
            "pre_mix_g": pre_mix_g, "post_mix_g": post_mix_g, "pre_mlp_g": pre_mlp_g,
            "post_mlp_g": post_mlp_g}

def first_block(x, w_in, w_dw, b_dw, conv_ln_g, conv_ln_b, rpb, w_out, w_up, w_down,
              pre_mix_g, post_mix_g, pre_mlp_g, post_mlp_g):
    splits = [CONV_WIDTH, 2 * CONV_WIDTH, 2 * CONV_WIDTH + NA_WIDTH, 2 * CONV_WIDTH + 2 * NA_WIDTH]
    for l in range(DEPTH):
        h = rms_norm(x, pre_mix_g[l])
        proj = h @ w_in[l]
        a, gate, q, k, v = jnp.split(proj, splits, axis=-1)
        yc = conformer_conv_group(a, gate, w_dw[l], b_dw[l], conv_ln_g[l], conv_ln_b[l])
        ya = neighbourhood_attention_group(q, k, v, rpb[l])
        mix = jnp.concatenate([yc, ya], axis=-1) @ w_out[l]
        x = x + rms_norm(mix, post_mix_g[l])
        h = rms_norm(x, pre_mlp_g[l])
        f = jnp.square(jax.nn.relu(h @ w_up[l])) @ w_down[l]
        x = x + rms_norm(f, post_mlp_g[l])
    return x


MLA_HEADS = 16
Q_LORA = 512
KV_LORA = 512
QK_NOPE = 128
QK_ROPE = 64
V_HEAD = 128
QK_HEAD = QK_NOPE + QK_ROPE
ROPE_THETA = 10000.0
Q_BLOCK = 128
SGU_WIDTH = D_MODEL
SGU_GROUPS = 8
SGU_GROUP_DIM = SGU_WIDTH // SGU_GROUPS
CHUNK = 128
PEER_HEADS = 8
N_KEYS = 128
N_EXPERTS = N_KEYS * N_KEYS
PEER_TOPK = 16
KEY_DIM = 128
TOKEN_BLOCK = 128
EPS = 1e-6

OFF_CQ = Q_LORA
OFF_CKV = OFF_CQ + KV_LORA
OFF_KPE = OFF_CKV + QK_ROPE
OFF_SGU = OFF_KPE + 2 * SGU_WIDTH
IN_COLS_2 = OFF_SGU + 2 * D_MODEL


def rmsnorm(x, g):
    xf = x.astype(jnp.float32)
    r = lax.rsqrt(jnp.mean(xf * xf, axis=-1, keepdims=True) + EPS)
    return (xf * r).astype(x.dtype) * g

def layernorm(x, g, b):
    xf = x.astype(jnp.float32)
    mu = jnp.mean(xf, axis=-1, keepdims=True)
    var = jnp.mean(jnp.square(xf - mu), axis=-1, keepdims=True)
    return ((xf - mu) * lax.rsqrt(var + EPS)).astype(x.dtype) * g + b

def rope(x, positions):
    d = x.shape[-1]
    freqs = ROPE_THETA ** (-jnp.arange(0, d, 2, dtype=jnp.float32) / d)
    ang = positions.astype(jnp.float32)[..., None] * freqs
    cos = jnp.cos(ang)[:, :, None, :].astype(x.dtype)
    sin = jnp.sin(ang)[:, :, None, :].astype(x.dtype)
    x1, x2 = x[..., : d // 2], x[..., d // 2 :]
    return jnp.concatenate([x1 * cos - x2 * sin, x1 * sin + x2 * cos], axis=-1)

def causal_block_attention(q, k, v):
    B, S, H, Dq = q.shape
    Dv = v.shape[-1]
    nb = S // Q_BLOCK
    qb = q.reshape(B, nb, Q_BLOCK, H, Dq).transpose(1, 0, 2, 3, 4)
    key_pos = jnp.arange(S)
    scale = Dq ** -0.5

    def one_block(args):
        q_blk, blk = args
        s = jnp.einsum("bqhd,bkhd->bhqk", q_blk, k).astype(jnp.float32) * scale
        q_pos = blk * Q_BLOCK + jnp.arange(Q_BLOCK)
        mask = q_pos[:, None] >= key_pos[None, :]
        s = jnp.where(mask[None, None], s, -jnp.inf)
        p = jax.nn.softmax(s, axis=-1).astype(v.dtype)
        return jnp.einsum("bhqk,bkhd->bqhd", p, v)

    o = lax.map(one_block, (qb, jnp.arange(nb)))
    return o.transpose(1, 0, 2, 3, 4).reshape(B, S, H * Dv)

def mla_branch(c_q, c_kv, k_pe, positions, g_q_a, w_uq, g_kv_a, w_ukv):
    B, S, _ = c_q.shape
    q = jnp.einsum("bsr,rhd->bshd", rmsnorm(c_q, g_q_a), w_uq)
    q = jnp.concatenate([q[..., :QK_NOPE], rope(q[..., QK_NOPE:], positions)], axis=-1)
    kv = jnp.einsum("bsr,rhd->bshd", rmsnorm(c_kv, g_kv_a), w_ukv)
    k_nope, v = kv[..., :QK_NOPE], kv[..., QK_NOPE:]
    k_pe = rope(k_pe[:, :, None, :], positions)
    k = jnp.concatenate([k_nope, jnp.broadcast_to(k_pe, (B, S, MLA_HEADS, QK_ROPE))], axis=-1)
    return causal_block_attention(q, k, v)

def sgu_branch(z, ln_g, ln_b, w_spatial, b_spatial):
    z = jax.nn.gelu(z)
    u, v = z[..., :SGU_WIDTH], z[..., SGU_WIDTH:]
    v = layernorm(v, ln_g, ln_b)
    B, S, _ = v.shape
    vg = v.reshape(B, S // CHUNK, CHUNK, SGU_GROUPS, SGU_GROUP_DIM)
    w = w_spatial * jnp.tril(jnp.ones((CHUNK, CHUNK), dtype=w_spatial.dtype))[None]
    mixed = jnp.einsum("gts,bcsgd->bctgd", w, vg) + b_spatial.T[None, None, :, :, None]
    return u * mixed.reshape(B, S, SGU_WIDTH)

def peer_ffn(h, w_pq, peer_keys, peer_u, peer_v):
    B, S, D = h.shape
    q = jnp.einsum("bsd,dhk->bshk", h, w_pq).reshape(B, S, PEER_HEADS, 2, KEY_DIM)
    sub = jnp.einsum("bshpk,hpnk->bshpn", q, peer_keys).astype(jnp.float32)
    s, i = lax.top_k(sub, PEER_TOPK)
    cand = (s[..., 0, :, None] + s[..., 1, None, :]).reshape(B, S, PEER_HEADS, PEER_TOPK * PEER_TOPK)
    cidx = (i[..., 0, :, None] * N_KEYS + i[..., 1, None, :]).reshape(B, S, PEER_HEADS, PEER_TOPK * PEER_TOPK)
    top_s, pos = lax.top_k(cand, PEER_TOPK)
    idx = jnp.take_along_axis(cidx, pos, axis=-1)
    gate = jax.nn.softmax(top_s, axis=-1).astype(h.dtype)
    nt = (B * S) // TOKEN_BLOCK
    hb = h.reshape(nt, TOKEN_BLOCK, D)
    ib = idx.reshape(nt, TOKEN_BLOCK, PEER_HEADS, PEER_TOPK)
    gb = gate.reshape(nt, TOKEN_BLOCK, PEER_HEADS, PEER_TOPK)

    def one_block(args):
        x_blk, i_blk, g_blk = args
        u = jnp.take(peer_u, i_blk, axis=0)
        a = jax.nn.gelu(jnp.einsum("td,thkd->thk", x_blk, u)) * g_blk
        v = jnp.take(peer_v, i_blk, axis=0)
        return jnp.einsum("thk,thkd->td", a, v)

    return lax.map(one_block, (hb, ib, gb)).reshape(B, S, D)

def second_inputs(seed: int = 0) -> dict:
    key = jax.random.key(seed)
    ks = jax.random.split(key, 24)
    f32 = jnp.float32
    nrm = lambda k, shape, scale: jax.random.normal(k, shape, f32) * scale
    gain = lambda k, shape: 1.0 + 0.05 * jax.random.normal(k, shape, f32)
    L = DEPTH
    x = jax.random.normal(ks[0], (BATCH, SEQ, D_MODEL), f32)
    offsets = jax.random.randint(ks[1], (BATCH, 1), 0, 4096, dtype=jnp.int32)
    positions = offsets + jnp.arange(SEQ, dtype=jnp.int32)[None, :]
    return {
        "x": x,
        "positions": positions,
        "g_norm1": gain(ks[2], (L, D_MODEL)),
        "w_in": nrm(ks[3], (L, D_MODEL, IN_COLS_2), D_MODEL ** -0.5),
        "g_q_a": gain(ks[4], (L, Q_LORA)),
        "w_uq": nrm(ks[5], (L, Q_LORA, MLA_HEADS, QK_HEAD), Q_LORA ** -0.5),
        "g_kv_a": gain(ks[6], (L, KV_LORA)),
        "w_ukv": nrm(ks[7], (L, KV_LORA, MLA_HEADS, QK_NOPE + V_HEAD), KV_LORA ** -0.5),
        "sgu_ln_g": gain(ks[8], (L, SGU_WIDTH)),
        "sgu_ln_b": nrm(ks[9], (L, SGU_WIDTH), 0.02),
        "w_spatial": nrm(ks[10], (L, SGU_GROUPS, CHUNK, CHUNK), CHUNK ** -0.5),
        "b_spatial": gain(ks[11], (L, SGU_GROUPS, CHUNK)),
        "b_gate": nrm(ks[12], (L, 2 * D_MODEL), 0.01),
        "w_out": nrm(ks[13], (L, D_MODEL, D_MODEL), D_MODEL ** -0.5),
        "g_norm2": gain(ks[14], (L, D_MODEL)),
        "w_peer_q": nrm(ks[15], (L, D_MODEL, PEER_HEADS, 2 * KEY_DIM), D_MODEL ** -0.5),
        "peer_keys": nrm(ks[16], (L, PEER_HEADS, 2, N_KEYS, KEY_DIM), KEY_DIM ** -0.5),
        "peer_u": nrm(ks[17], (L, N_EXPERTS, D_MODEL), D_MODEL ** -0.5),
        "peer_v": nrm(ks[18], (L, N_EXPERTS, D_MODEL), PEER_HEADS ** -0.5),
        "g_final": gain(ks[19], (D_MODEL,)),
    }

def second_block(x, positions, g_norm1, w_in, g_q_a, w_uq, g_kv_a, w_ukv, sgu_ln_g, sgu_ln_b,
              w_spatial, b_spatial, b_gate, w_out, g_norm2, w_peer_q, peer_keys, peer_u,
              peer_v, g_final):
    for l in range(DEPTH):
        h = rmsnorm(x, g_norm1[l])
        proj = h @ w_in[l]
        c_q = proj[..., :OFF_CQ]
        c_kv = proj[..., OFF_CQ:OFF_CKV]
        k_pe = proj[..., OFF_CKV:OFF_KPE]
        z_sgu = proj[..., OFF_KPE:OFF_SGU]
        gates = jax.nn.sigmoid(proj[..., OFF_SGU:] + b_gate[l])
        o_a = mla_branch(c_q, c_kv, k_pe, positions, g_q_a[l], w_uq[l], g_kv_a[l], w_ukv[l])
        o_b = sgu_branch(z_sgu, sgu_ln_g[l], sgu_ln_b[l], w_spatial[l], b_spatial[l])
        merged = gates[..., :D_MODEL] * o_a + gates[..., D_MODEL:] * o_b
        x = x + merged @ w_out[l]
        h2 = rmsnorm(x, g_norm2[l])
        x = x + peer_ffn(h2, w_peer_q[l], peer_keys[l], peer_u[l], peer_v[l])
    return rmsnorm(x, g_final)


def setup_inputs(seed=0):
    out = dict(first_inputs(seed))
    for name, value in second_inputs(seed + 1).items():
        if name != "x":
            out[name + "_2"] = value
    return out


def reference(
    x, w_in, w_dw, b_dw, conv_ln_g, conv_ln_b, rpb, w_out, w_up, w_down, pre_mix_g, post_mix_g,
    pre_mlp_g, post_mlp_g, positions_2, g_norm1_2, w_in_2, g_q_a_2, w_uq_2, g_kv_a_2, w_ukv_2,
    sgu_ln_g_2, sgu_ln_b_2, w_spatial_2, b_spatial_2, b_gate_2, w_out_2, g_norm2_2, w_peer_q_2,
    peer_keys_2, peer_u_2, peer_v_2, g_final_2,
):
    x = first_block(
        x, w_in, w_dw, b_dw, conv_ln_g, conv_ln_b, rpb, w_out, w_up, w_down, pre_mix_g,
        post_mix_g, pre_mlp_g, post_mlp_g,
    )
    return second_block(
        x, positions_2, g_norm1_2, w_in_2, g_q_a_2, w_uq_2, g_kv_a_2, w_ukv_2, sgu_ln_g_2,
        sgu_ln_b_2, w_spatial_2, b_spatial_2, b_gate_2, w_out_2, g_norm2_2, w_peer_q_2,
        peer_keys_2, peer_u_2, peer_v_2, g_final_2,
    )


_drawn_inputs = setup_inputs


def setup_inputs(seed=0):
    import zlib

    import numpy as np

    out = dict(_drawn_inputs(seed))
    spreads = {}
    factors = {'b_dw': 3.148,
     'conv_ln_b': 4.581,
     'rpb': 6.706,
     'g_norm1_2': 2.685,
     'g_q_a_2': 8.0,
     'g_kv_a_2': 5.564,
     'sgu_ln_g_2': 5.312,
     'sgu_ln_b_2': 26.381,
     'b_spatial_2': 3.853,
     'b_gate_2': 22.818,
     'g_norm2_2': 8.0}
    for name, (base, spread) in spreads.items():
        noise = np.random.default_rng([zlib.crc32(name.encode()), seed]).standard_normal(out[name].shape)
        drawn = base * np.exp(spread * noise) if base else spread * noise
        out[name] = __import__('jax').numpy.asarray(drawn.astype(out[name].dtype))
    for name, factor in factors.items():
        out[name] = (out[name] * factor).astype(out[name].dtype)
    return out
```

```python
from contextlib import ExitStack

import concourse.bass as bass
import numpy as np
from concourse import mybir

F32 = mybir.dt.float32
F32R = mybir.dt.float32r
I32 = mybir.dt.int32
U32 = mybir.dt.uint32
ACT = mybir.ActivationFunctionType
ALU = mybir.AluOpType
AX = mybir.AxisListType

P = 128
T = 256
NH = T // P
D = 2048
DC = D // P
CW = D // 2
CC = CW // P
TAPS = 31
PADT = T + TAPS - 1
HEADS, HD = 16, 64
GRID_W, WR, WC = 64, 8, 16
ROWS = T // GRID_W
FF = 4 * D
QUARTERS = FF // D
LORA, NOPE, ROPE, VH = 512, 128, 64, 128
QK = NOPE + ROPE
LC = LORA // P
GROUPS, GD = 8, 256
PH, NKEYS, TOPK = 8, 128, 16
PICKS = PH * TOPK
RING = 4
GR = 8
NEG = -1e30

C_ID, C_NA, C_CAUSAL, C_TRIL, C_FREQ, C_IOTA = 0, 128, 384, 512, 640, 672
C_ALL = 688

VECS = [("pre_mix_g", DC), ("pre_mlp_g", DC), ("g_norm1_2", DC), ("g_norm2_2", DC), ("conv_ln_g", CC),
        ("conv_ln_b", CC), ("b_dw", CC), ("g_q_a_2", LC), ("g_kv_a_2", LC), ("b_spatial_2", GROUPS)]
VEC_AT = {}
_at = 0
for _name, _n in VECS:
    VEC_AT[_name] = _at
    _at += _n
VEC_ROWS = _at


def shape_constants():
    c = np.zeros((P, C_ALL), np.float32)
    i, j = np.arange(P)[:, None], np.arange(P)[None, :]
    c[:, C_ID:C_ID + P] = i == j
    col, key = np.arange(P)[:, None] % GRID_W, np.arange(T)[None, :] % GRID_W
    start = np.clip(col - WC // 2, 0, GRID_W - WC)
    window = np.where((key >= start) & (key < start + WC), 0.0, NEG)
    c[:, C_NA:C_NA + T] = window.reshape(P, ROWS, GRID_W)[:, :, ::-1].reshape(P, T)
    c[:, C_CAUSAL:C_CAUSAL + P] = np.where(j <= i, 0.0, NEG)
    c[:, C_TRIL:C_TRIL + P] = i <= j
    half = ROPE // 2
    c[:, C_FREQ:C_FREQ + half] = 10000.0 ** (-np.arange(0, ROPE, 2) / ROPE)
    c[:, C_IOTA:C_IOTA + TOPK] = np.arange(TOPK)
    return c


class Steps:

    def __init__(self, eng, sem, start=0):
        self.eng, self.sem, self.start, self.n = eng, sem, start, 0

    def __call__(self, instruction):
        instruction.then_inc(self.sem, 1)
        self.n += 1
        self.eng.wait_ge(self.sem, self.start + self.n)


class Core:

    def __init__(self, nc, ctx):
        self.nc, self.stage = nc, 0
        self.past = []
        self.tiles = 0
        self.outs = 0

        def sem(name):
            return ctx.enter_context(nc.semaphore(name))

        self.at = (nc.sbuf_base + 31) // 32 * 32
        sb = self.place
        self.const = sb("const", [P, C_ALL])
        self.x = sb("x", [P, NH, D])
        self.vec = sb("vec", [P, VEC_ROWS])
        self.ring = sb("ring", [P, RING, 4, 512])
        self.wh = sb("wh", [P, 2, 4, 512], F32R)
        self.wl = sb("wl", [P, 2, 4, 512], F32R)
        self.th = sb("th", [P, DC, T], F32R)
        self.tl = sb("tl", [P, DC, T], F32R)
        self.small = sb("small", [P, 64])
        self.ps = ctx.enter_context(nc.psum_tensor("ps", [P, 8, 512], F32))
        self.landed = [sem(f"slab_landed{i}") for i in range(RING)]
        self.high_ready = sem("high_ready")
        self.low_ready = sem("low_ready")
        self.slabs_used = sem("slabs_used")
        self.outs_free = sem("outs_free")
        self.ident = self.const[:, C_ID:C_ID + P]
        self.arena = self.at

    def place(self, name, shape, dt=F32, at=None):
        at = self.at if at is None else self.arena + at
        size = 4 * int(np.prod(shape[1:]))
        self.at = at + (size + 31) // 32 * 32
        return self.nc.alloc_sbuf_tensor_at(name, shape, dt, offset=at)

    def scratch(self, at, *buffers):
        self.at = self.arena + at
        return [self.place(f"{b[0]}_{self.stage}", *b[1:]) for b in buffers]

    def v(self, name, chunk=0, n=1):
        return self.vec[:, VEC_AT[name] + chunk:VEC_AT[name] + chunk + n]

    def new(self, *names):
        self.stage += 1
        sems = [self.nc.alloc_semaphore(f"{n}_{self.stage}") for n in names]
        self.past += sems
        return sems

    def clear_semaphores(self):
        with self.nc.Block():
            self.nc.clear_and_free_semaphores(self.past)
        self.past = []

    def v(self, name, chunk=0, n=1):
        return self.vec[:, VEC_AT[name] + chunk:VEC_AT[name] + chunk + n]

    def new(self, *names):
        self.stage += 1
        sems = [self.nc.alloc_semaphore(f"{n}_{self.stage}") for n in names]
        self.past += sems
        return sems

    def clear_semaphores(self):
        ids = sorted(int(s.num) for s in self.past)
        with self.nc.Block() as block:

            @block.gpsimd
            def _(pool):
                first = 0
                for n in range(1, len(ids) + 1):
                    if n == len(ids) or ids[n] != ids[n - 1] + 1:
                        pool.sem_clear(range(ids[first], ids[n - 1] + 1))
                        first = n

        for s in self.past:
            self.nc.release_semaphore(s)
        self.past = []


    def load_slab(self, sp, dma, tile, i, first=False):
        if not first:
            sp.wait_ge(self.low_ready, (tile - 1) * RING + (i + 1))
        src = dma(i)
        sp.dma_start(self.ring[:, i, :, 0:src.shape[-1]], src).then_inc(self.landed[i], 16)

    def split_high(self, act, tile, i, w=512):
        act.wait_ge(self.landed[i], tile * 16 + 16)
        act.wait_ge(self.slabs_used, tile * RING + (i + 1))
        self.nc.scalar.copy(self.wh[:, i % 2, :, 0:w], self.ring[:, i, :, 0:w]).then_inc(self.high_ready, 1)

    def split_low(self, dve, tile, i, w=512):
        dve.wait_ge(self.high_ready, tile * RING + (i + 1))
        self.nc.vector.tensor_tensor(self.wl[:, i % 2, :, 0:w], self.ring[:, i, :, 0:w],
                                     self.wh[:, i % 2, :, 0:w].bitcast(F32), ALU.subtract).then_inc(self.low_ready, 1)

    def multiply_slab(self, pe, tile, i, out, th, tl, chunk, start, stop, w=512):
        pe.wait_ge(self.low_ready, tile * RING + (i + 1))
        mm = self.nc.tensor.matmul
        for k in range(4):
            for half in range(NH):
                hi = th[:, chunk + k, half * P:(half + 1) * P]
                lo = tl[:, chunk + k, half * P:(half + 1) * P]
                wh, wl = self.wh[:, i % 2, k, 0:w], self.wl[:, i % 2, k, 0:w]
                o = self.ps[:, out + half, 0:w]
                mm(o, hi, wh, start=start and k == 0, stop=False)
                mm(o, hi, wl, start=False, stop=False)
                last = mm(o, lo, wh, start=False, stop=stop and k == 3)
        last.then_inc(self.slabs_used, 1)


def tile_view(w, col, width=512):
    rows = w.rearrange("(s c p) n -> s p c n", c=4, p=P)

    def slab(i):
        return rows[i, :, :, bass.ds(col, width)]

    return slab


def over_tiles(eng, n, body):
    body(0, 0)
    pairs = (n - 2) // 2
    if pairs > 1:
        with eng.Fori(0, pairs) as t:
            body(t * 2 + 1, 1)
            body(t * 2 + 2, 0)
    elif pairs == 1:
        body(1, 1)
        body(2, 0)
    for tile in range(2 * max(pairs, 0) + 1, n):
        body(tile, tile % 2)


def dense(core, name, n, source, evacuate, nexts, w=512, dve_slab=None, before=None):
    nc, base, outs = core.nc, core.tiles, core.outs
    with nc.Block() as block:

        @block.sync
        def _(sp):
            if before is not None:
                before(sp)
            if n > 1:
                with sp.Fori(1, n) as t:
                    for i in range(RING):
                        core.load_slab(sp, source(t), t + base, i)
            if nexts is not None:
                for i in range(RING):
                    core.load_slab(sp, nexts, base + n, i)

        @block.tensor
        def _(pe):
            def tile(t, parity):
                pe.wait_ge(core.outs_free, (t + outs) * 2 + 2)
                for i in range(RING):
                    core.multiply_slab(pe, t + base, i, 2 * parity, core.th, core.tl, 4 * i,
                                       i == 0, i == RING - 1, w)

            if n >= 4:
                with pe.Fori(0, n // 2) as t:
                    tile(t * 2, 0)
                    tile(t * 2 + 1, 1)
                if n % 2:
                    tile(n - 1, 0)
            else:
                for t in range(n):
                    tile(t, t % 2)

        @block.scalar
        def _(act):
            def read_out(t, parity):
                act.wait_ge(core.slabs_used, (t + base) * RING + (RING + 2))
                for half in range(NH):
                    evacuate(act, t, half, core.ps[:, 2 * parity + half, 0:w]).then_inc(core.outs_free, 1)

            def tile(t, parity):
                for i in range(RING):
                    core.split_high(act, t + base, i, w)
                    if i == 0 and not (isinstance(t, int) and t == 0):
                        read_out(t - 1, 1 - parity)

            over_tiles(act, n, tile)
            read_out(n - 1, (n - 1) % 2)

        @block.vector
        def _(dve):
            if dve_slab is None:
                with dve.Fori(0, n) as t:
                    for i in range(RING):
                        core.split_low(dve, t + base, i, w)
            else:
                for t in range(n):
                    for i in range(RING):
                        core.split_low(dve, t + base, i, w)
                        dve_slab(dve, t * RING + i)

    core.tiles += n
    core.outs += n


def transpose_split(core, src, chunks, hi, lo, sems, scale=None):
    nc = core.nc
    turned, high, low = sems

    def psum(c):
        return core.ps[:, 4 + c % 4, 0:T]

    def pe_part(pe):
        for c in range(chunks):
            if c >= 4:
                pe.wait_ge(low, c - 3)
            for half in range(NH):
                last = nc.tensor.transpose(psum(c)[:, half * P:(half + 1) * P],
                                           src[:, half, c * P:(c + 1) * P], core.ident)
            last.then_inc(turned, 1)

    def act_part(act):
        for c in range(chunks):
            act.wait_ge(turned, c + 1)
            kw = {} if scale is None else {"scale": scale(c)}
            nc.scalar.activation(hi[:, c, :], psum(c), ACT.Copy, **kw).then_inc(high, 1)

    def dve_part(dve):
        for c in range(chunks):
            dve.wait_ge(high, c + 1)
            h = hi[:, c, :].bitcast(F32)
            if scale is None:
                nc.vector.tensor_tensor(lo[:, c, :], psum(c), h, ALU.subtract).then_inc(low, 1)
            else:
                nc.vector.scalar_tensor_tensor(out=lo[:, c, :], in0=psum(c), scalar=scale(c), in1=h,
                                               op0=ALU.mult, op1=ALU.subtract).then_inc(low, 1)

    return pe_part, act_part, dve_part


def rms_factor(nc, dve, step, ms, out, tmp, width, eps, mean_ready, rooted, k):
    nc.vector.tensor_scalar(ms, ms, 1.0 / width, eps, ALU.mult, ALU.add).then_inc(mean_ready, 1)
    dve.wait_ge(rooted, k)
    step(nc.vector.reciprocal(out, tmp))
    step(nc.vector.tensor_tensor(tmp, out, out, ALU.mult))
    step(nc.vector.tensor_tensor(tmp, tmp, ms, ALU.mult))
    step(nc.vector.tensor_scalar(tmp, tmp, -0.5, 1.5, ALU.mult, ALU.add))
    step(nc.vector.tensor_tensor(out, out, tmp, ALU.mult))


def norm_stage(core, y, eps, buf, scratch, post_gain=None, post_eps=None, gain_name=None, token_gain=None, out=None):
    nc, x = core.nc, core.x
    with ExitStack() as local:
        core.local = local
        done, sums, mean_ready, rooted, added, scaled, turned, high, low, loaded, stored = core.new(
            "dve_done", "sums_ready", "mean_ready", "rooted", "x_ready", "normed", "turned", "high", "low",
            "gain_loaded", "stored")
        gains, = core.scratch(scratch, ("gain_rows", [P, D]))
        ms, rf, tmp = core.small[:, 0:2], core.small[:, 2:4], core.small[:, 4:6]
        pe_part, act_part, dve_part = transpose_split(
            core, buf, DC, core.th, core.tl, (turned, high, low),
            (lambda c: core.v(gain_name, c)) if gain_name else None)
        rounds = ([(y, post_eps)] if post_gain is not None else []) + [(x, eps)]
        gain = post_gain if post_gain is not None else token_gain
        block = local.enter_context(nc.Block())

        @block.sync
        def _(sp):
            if gain is not None:
                sp.dma_start(gains[:], gain.partition_broadcast(P)).then_inc(loaded, 16)
            if out is not None:
                sp.wait_ge(scaled, NH)
                sp.dma_start(out.rearrange("(h p) d -> p h d", p=P), buf[:]).then_inc(stored, 16)
                sp.wait_ge(stored, 16)

        @block.scalar
        def _(act):
            for r, (src, _) in enumerate(rounds):
                if src is x and y is not None:
                    act.wait_ge(added, 1)
                for half in range(NH):
                    nc.scalar.activation(buf[:, half, :], src[:, half, :], ACT.Square,
                                         accum_out=ms[:, half:half + 1]).then_inc(sums, 1)
                act.wait_ge(mean_ready, r + 1)
                nc.scalar.activation(tmp, ms, ACT.Sqrt).then_inc(rooted, 1)
            if out is None:
                act_part(act)

        @block.vector
        def _(dve):
            step = Steps(dve, done)
            if y is not None and post_gain is None:
                nc.vector.tensor_tensor(x[:], x[:], y[:], ALU.add).then_inc(added, 1)
            for r, (src, e) in enumerate(rounds):
                dve.wait_ge(sums, 2 * r + 2)
                rms_factor(nc, dve, step, ms, rf, tmp, D, e, mean_ready, rooted, r + 1)
                if post_gain is not None and r == 0:
                    dve.wait_ge(loaded, 16)
                    for half in range(NH):
                        step(nc.vector.scalar_tensor_tensor(out=buf[:, half, :], in0=y[:, half, :],
                                                            scalar=rf[:, half:half + 1], in1=gains[:],
                                                            op0=ALU.mult, op1=ALU.mult))
                    nc.vector.tensor_tensor(x[:], x[:], buf[:], ALU.add).then_inc(added, 1)
            if token_gain is not None:
                dve.wait_ge(loaded, 16)
            for half in range(NH):
                factor = rf[:, half:half + 1]
                if token_gain is not None:
                    ins = nc.vector.scalar_tensor_tensor(out=buf[:, half, :], in0=x[:, half, :], scalar=factor,
                                                         in1=gains[:], op0=ALU.mult, op1=ALU.mult)
                else:
                    ins = nc.vector.tensor_scalar(buf[:, half, :], x[:, half, :], factor, None, ALU.mult)
                ins.then_inc(scaled, 1)
            if out is None:
                dve_part(dve)

        @block.tensor
        def _(pe):
            if out is None:
                pe.wait_ge(scaled, NH)
                pe_part(pe)


def setup_stage(core, ins, first):
    nc = core.nc
    with ExitStack() as local:
        core.local = local
        const_in, rows_in, x_in, turned, copied = core.new("const_in", "rows_in", "x_in", "turned", "copied")
        rows, = core.scratch(0, ("vec_rows", [VEC_ROWS, P]))
        block = local.enter_context(nc.Block())

        @block.sync
        def _(sp):
            sp.dma_start(core.const[:], ins["shape_constants"]).then_inc(const_in, 16)
            sp.dma_start(core.x[:], ins["x"][0].rearrange("(h p) d -> p h d", p=P)).then_inc(x_in, 16)
            for i in range(RING):
                core.load_slab(sp, first, 0, i, first=True)
            sp.wait_ge(x_in, 16)

        @block.tensor
        def _(pe):
            pe.wait_ge(const_in, 16)
            pe.wait_ge(rows_in, 16 * len(VECS))
            nc.tensor.transpose(core.ps[:, 0, 0:VEC_ROWS], rows[:], core.ident[0:VEC_ROWS, 0:VEC_ROWS]).then_inc(turned, 1)

        @block.scalar
        def _(act):
            for name, n in VECS:
                at = VEC_AT[name]
                src = ins[name][0]
                if len(src.shape) == 1:
                    src = src.rearrange("(c p) -> c p", p=P)
                act.dma_start(rows[at:at + n, :], src).then_inc(rows_in, 16)

        @block.vector
        def _(dve):
            nc.vector.memset(core.small[:, 0:1], 0.0).then_inc(core.slabs_used, 2)
            nc.vector.memset(core.small[:, 1:2], 0.0).then_inc(core.outs_free, 4)
            dve.wait_ge(turned, 1)
            nc.vector.tensor_copy(core.vec[:], core.ps[:, 0, 0:VEC_ROWS]).then_inc(copied, 1)


def gated_stage(core, glu, ut):
    nc = core.nc
    with ExitStack() as local:
        core.local = local
        gates, gated, turned, read, pads = core.new("gates_ready", "gated", "turned", "read", "pads")
        block = local.enter_context(nc.Block())
        side = (TAPS - 1) // 2

        @block.scalar
        def _(act):
            for half in range(NH):
                nc.scalar.activation(glu[:, half, CW:], glu[:, half, CW:], ACT.Sigmoid).then_inc(gates, 1)
            for c in range(CC):
                act.wait_ge(turned, c + 1)
                nc.scalar.copy(ut[:, c, side:side + T], core.ps[:, 4 + c % 4, 0:T]).then_inc(read, 1)

        @block.vector
        def _(dve):
            for half in range(NH):
                dve.wait_ge(gates, half + 1)
                nc.vector.tensor_tensor(glu[:, half, :CW], glu[:, half, :CW], glu[:, half, CW:], ALU.mult).then_inc(gated, 1)

        @block.gpsimd
        def _(pool):
            nc.gpsimd.memset(ut[:, :, 0:side], 0.0).then_inc(pads, 1)
            nc.gpsimd.memset(ut[:, :, side + T:], 0.0).then_inc(pads, 1)

        @block.tensor
        def _(pe):
            pe.wait_ge(gated, NH)
            for c in range(CC):
                if c >= 4:
                    pe.wait_ge(read, c - 3)
                for half in range(NH):
                    last = nc.tensor.transpose(core.ps[:, 4 + c % 4, half * P:(half + 1) * P],
                                               glu[:, half, c * P:(c + 1) * P], core.ident)
                last.then_inc(turned, 1)


def conv_norm_stage(core, conv, xc, sq, stat, scratch):
    nc = core.nc
    flat = "p c t -> p (c t)"
    with ExitStack() as local:
        core.local = local
        ones_in, mean, centred, squared, var, var_in, rooted, normed, sig, act_out, high, low, done = core.new(
            "ones_in", "mean", "centred", "squared", "var", "var_in", "rooted", "normed", "sigmoid",
            "silu_ready", "high", "low", "dve_done")
        ones, = core.scratch(scratch, ("ones", [P, P]))
        block = local.enter_context(nc.Block())
        v_, r_, t_ = stat[:, 0, :], stat[:, 1, :], stat[:, 2, :]

        @block.gpsimd
        def _(pool):
            nc.gpsimd.memset(ones[:], 1.0 / CW).then_inc(ones_in, 1)

        @block.tensor
        def _(pe):
            pe.wait_ge(ones_in, 1)
            for c in range(CC):
                last = nc.tensor.matmul(core.ps[:, 4, 0:T], ones[:], conv[:, c, :], start=c == 0, stop=c == CC - 1)
            last.then_inc(mean, 1)
            for c in range(CC):
                pe.wait_ge(squared, c + 1)
                last = nc.tensor.matmul(core.ps[:, 5, 0:T], ones[:], sq[:, c, :], start=c == 0, stop=c == CC - 1)
            last.then_inc(var, 1)

        @block.scalar
        def _(act):
            for c in range(CC):
                act.wait_ge(centred, c + 1)
                nc.scalar.activation(sq[:, c, :], xc[:, c, :], ACT.Square).then_inc(squared, 1)
            act.wait_ge(var_in, 1)
            nc.scalar.activation(t_, v_, ACT.Sqrt).then_inc(rooted, 1)
            for c in range(CC):
                act.wait_ge(normed, c + 1)
                nc.scalar.activation(sq[:, c, :], xc[:, c, :], ACT.Sigmoid, scale=core.v("conv_ln_g", c),
                                     bias=core.v("conv_ln_b", c)).then_inc(sig, 1)
            for c in range(CC):
                act.wait_ge(act_out, c + 1)
                nc.scalar.copy(core.th[:, c, :], conv[:, c, :]).then_inc(high, 1)

        @block.vector
        def _(dve):
            step = Steps(dve, done)
            dve.wait_ge(mean, 1)
            for c in range(CC):
                nc.vector.tensor_tensor(xc[:, c, :], conv[:, c, :], core.ps[:, 4, 0:T], ALU.subtract).then_inc(centred, 1)
            dve.wait_ge(var, 1)
            nc.vector.tensor_scalar(v_, core.ps[:, 5, 0:T], 1e-5, None, ALU.add).then_inc(var_in, 1)
            dve.wait_ge(rooted, 1)
            step(nc.vector.reciprocal(r_, t_))
            step(nc.vector.tensor_tensor(t_, r_, r_, ALU.mult))
            step(nc.vector.tensor_tensor(t_, t_, v_, ALU.mult))
            step(nc.vector.tensor_scalar(t_, t_, -0.5, 1.5, ALU.mult, ALU.add))
            step(nc.vector.tensor_tensor(r_, r_, t_, ALU.mult))
            for c in range(CC):
                nc.vector.tensor_tensor(xc[:, c, :], xc[:, c, :], r_, ALU.mult).then_inc(normed, 1)
            for c in range(CC):
                dve.wait_ge(sig, c + 1)
                step(nc.vector.tensor_scalar(xc[:, c, :], xc[:, c, :], core.v("conv_ln_g", c),
                                             core.v("conv_ln_b", c), ALU.mult, ALU.add))
                nc.vector.tensor_tensor(conv[:, c, :], xc[:, c, :], sq[:, c, :], ALU.mult).then_inc(act_out, 1)
            for c in range(CC):
                dve.wait_ge(high, c + 1)
                nc.vector.tensor_tensor(core.tl[:, c, :], conv[:, c, :], core.th[:, c, :].bitcast(F32),
                                        ALU.subtract).then_inc(low, 1)


def turn_stage(core, src, chunks, out_for):
    nc = core.nc
    with ExitStack() as local:
        core.local = local
        turned, even_read, odd_read = core.new("turned", "even_read", "odd_read")
        block = local.enter_context(nc.Block())

        @block.tensor
        def _(pe):
            for c in range(chunks):
                if c >= 4:
                    pe.wait_ge(odd_read if c % 2 else even_read, c // 2 - 1)
                for half in range(NH):
                    last = nc.tensor.transpose(core.ps[:, 4 + c % 4, half * P:(half + 1) * P],
                                               src[:, half, c * P:(c + 1) * P], core.ident)
                last.then_inc(turned, 1)

        @block.scalar
        def _(act):
            for c in range(0, chunks, 2):
                act.wait_ge(turned, c + 1)
                nc.scalar.copy(out_for(c), core.ps[:, 4 + c % 4, 0:T]).then_inc(even_read, 1)

        @block.vector
        def _(dve):
            for c in range(1, chunks, 2):
                dve.wait_ge(turned, c + 1)
                nc.vector.tensor_copy(out_for(c), core.ps[:, 4 + c % 4, 0:T]).then_inc(odd_read, 1)


def attention_stage(core, heads, scale, spans, mask, products, v_of, vw, out, scratch, turn=None, prepare=None):
    nc = core.nc
    width = sum(n for _, n in spans)
    blocks = [(half, k) for half, (_, n) in enumerate(spans) for k in range(n // P)]
    with ExitStack() as local:
        core.local = local
        (laid, laid_act, laid_dve, scored, masked, peaked, exps, turned, copied, mixed, normed, summed,
         ready) = core.new("qk_turned", "qk_by_act", "qk_by_dve", "scores_ready", "masked", "max_ready",
                           "probs_ready", "probs_turned", "probs_copied", "mixed", "normed", "inverted", "ready")
        s, p, pt, peak, total, inverse = core.scratch(
            scratch, ("scores_sb", [P, 2, width]), ("probs_sb", [P, 2, width]), ("probs_t", [P, 2, width]),
            ("peaks", [P, 2, 2]), ("totals", [P, heads, 2]), ("inverses", [P, heads, 2]))
        block = local.enter_context(nc.Block())
        lead = 1 if turn else 0
        rounds = range(heads + 2 + lead)

        @block.tensor
        def _(pe):
            for i in rounds:
                if turn and i < heads:
                    if i >= 1:
                        pe.wait_ge(laid_act, i)
                        pe.wait_ge(laid_dve, i)
                    for o, src in turn(i)[0]:
                        last = nc.tensor.transpose(o, src, core.ident)
                    last.then_inc(laid, 1)
                h = i - lead
                if 0 <= h < heads:
                    if turn:
                        pe.wait_ge(laid_act, h + 1)
                        pe.wait_ge(laid_dve, h + 1)
                    if h >= 2:
                        pe.wait_ge(masked, h - 1)
                    for half, (at, n) in enumerate(spans):
                        parts = products(h, half, n)
                        for j, (q, k) in enumerate(parts):
                            last = nc.tensor.matmul(core.ps[:, h % 2, at:at + n], q, k,
                                                    start=j == 0, stop=j == len(parts) - 1)
                    last.then_inc(scored, 1)
                h -= 1
                if 0 <= h < heads:
                    pe.wait_ge(exps, 2 * h + 2)
                    if h >= 2:
                        pe.wait_ge(copied, h - 1)
                    for half, k in blocks:
                        at = spans[half][0] + k * P
                        last = nc.tensor.transpose(core.ps[:, 2 + h % 2, at:at + P], p[:, h % 2, at:at + P], core.ident)
                    last.then_inc(turned, 1)
                h -= 1
                if 0 <= h < heads:
                    pe.wait_ge(copied, h + 1)
                    if h >= 2:
                        pe.wait_ge(normed, 2 * (h - 1))
                    for half, (at, n) in enumerate(spans):
                        for k in range(n // P):
                            last = nc.tensor.matmul(core.ps[:, 4 + h % 2, half * vw:(half + 1) * vw],
                                                    pt[:, h % 2, at + k * P:at + (k + 1) * P], v_of(h, k),
                                                    start=k == 0, stop=k == n // P - 1)
                    last.then_inc(mixed, 1)

        @block.scalar
        def _(act):
            for i in range(heads + lead):
                if turn and i < heads:
                    act.wait_ge(laid, i + 1)
                    if i >= 2:
                        act.wait_ge(scored, i - 1)
                    o, src = turn(i)[1]
                    nc.scalar.copy(o, src).then_inc(laid_act, 1)
                h = i - lead
                if 0 <= h < heads:
                    act.wait_ge(peaked, h + 1)
                    if h >= 2:
                        act.wait_ge(turned, h - 1)
                    for half, (at, n) in enumerate(spans):
                        nc.scalar.activation(p[:, h % 2, at:at + n], s[:, h % 2, at:at + n], ACT.Exp,
                                             bias=peak[:, h % 2, half:half + 1],
                                             accum_out=total[:, h, half:half + 1]).then_inc(exps, 1)

        @block.gpsimd
        def _(pool):
            if prepare:
                prepare(pool, ready)

        @block.vector
        def _(dve):
            if prepare:
                dve.wait_ge(ready, 1)
            for i in rounds:
                if turn and i < heads:
                    dve.wait_ge(laid, i + 1)
                    if i >= 2:
                        dve.wait_ge(scored, i - 1)
                    o, src = turn(i)[2]
                    nc.vector.tensor_copy(o, src).then_inc(laid_dve, 1)
                h = i - lead
                if 0 <= h < heads:
                    dve.wait_ge(scored, h + 1)
                    if h >= 2:
                        dve.wait_ge(exps, 2 * (h - 1))
                    m = mask(h)
                    o, b = s[:, h % 2, :], core.ps[:, h % 2, 0:width]
                    if len(m.shape) == 3:
                        o, b = (z.rearrange("p (h k) -> p h k", h=m.shape[1]) for z in (o, b))
                    nc.vector.scalar_tensor_tensor(out=o, in0=b, scalar=scale, in1=m, op0=ALU.mult,
                                                   op1=ALU.add).then_inc(masked, 1)
                    dve.wait_ge(masked, h + 1)
                    for half, (at, n) in enumerate(spans):
                        last = nc.vector.tensor_reduce(peak[:, h % 2, half:half + 1], s[:, h % 2, at:at + n],
                                                       AX.X, ALU.max, negate=True)
                    last.then_inc(peaked, 1)
                h -= 1
                if 0 <= h < heads:
                    dve.wait_ge(turned, h + 1)
                    if h >= 2:
                        dve.wait_ge(mixed, h - 1)
                    nc.vector.tensor_copy(pt[:, h % 2, :], core.ps[:, 2 + h % 2, 0:width]).then_inc(copied, 1)
                    nc.vector.reciprocal(inverse[:, h, :], total[:, h, :]).then_inc(summed, 1)
                h -= 1
                if 0 <= h < heads:
                    dve.wait_ge(mixed, h + 1)
                    dve.wait_ge(summed, h + 1)
                    for half in range(NH):
                        nc.vector.tensor_scalar(out[:, half, h * vw:(h + 1) * vw],
                                                core.ps[:, 4 + h % 2, half * vw:(half + 1) * vw],
                                                inverse[:, h, half:half + 1], None, ALU.mult).then_inc(normed, 1)


def split_stage(core, src, chunks, hi, lo, scale=None):
    nc = core.nc
    with ExitStack() as local:
        core.local = local
        pe_part, act_part, dve_part = transpose_split(core, src, chunks, hi, lo,
                                                      core.new("turned", "high", "low"), scale)
        block = local.enter_context(nc.Block())
        block.tensor(pe_part)
        block.scalar(act_part)
        block.vector(dve_part)


def mlp_stage(core, w_up, w_down, total, nexts, scratch):
    nc, base, outs = core.nc, core.tiles, core.outs
    up_rows = w_up.rearrange("(s c p) n -> s p c n", c=4, p=P)
    down_rows = w_down.rearrange("(s c p) n -> s p c n", c=4, p=P)
    NT = D // 512

    def up(q, n):
        return lambda i: up_rows[i, :, :, bass.ds(q * D + n * 512, 512)]

    def down(q, n):
        return lambda i: down_rows[q * 4 + i, :, :, n * 512:(n + 1) * 512]

    with ExitStack() as local:
        core.local = local
        cleared, squared, turned, f_high, f_low = core.new("cleared", "squared", "turned", "f_high", "f_low")
        fh, fl, relu, square = core.scratch(scratch, ("fh", [P, DC, T], F32R), ("fl", [P, DC, T], F32R),
                                            ("relu", [P, 2, NH, 512]), ("square", [P, 2, NH, 512]))
        block = local.enter_context(nc.Block())

        @block.sync
        def _(sp):
            def quarter(q, last):
                for n in range(1, NT):
                    for i in range(RING):
                        core.load_slab(sp, up(q, n), q * (2 * NT) + (base + n), i)
                for n in range(NT):
                    for i in range(RING):
                        core.load_slab(sp, down(q, n), q * (2 * NT) + (base + NT + n), i)
                for i in range(RING):
                    core.load_slab(sp, nexts if last else up(q + 1, 0), q * (2 * NT) + (base + 2 * NT), i)

            with sp.Fori(0, QUARTERS - 1) as q:
                quarter(q, False)
            quarter(QUARTERS - 1, True)

        @block.tensor
        def _(pe):
            def turn(q, n):
                pe.wait_ge(squared, q * (2 * NT) + 2 * n + 2)
                pe.wait_ge(f_low, q * (2 * NT) + 2 * n + 2)
                for half in range(NH):
                    for j in range(4):
                        last = nc.tensor.transpose(core.ps[:, 4 + half, j * P:(j + 1) * P],
                                                   square[:, n % 2, half, j * P:(j + 1) * P], core.ident)
                    last.then_inc(turned, 1)

            with pe.Fori(0, QUARTERS) as q:
                for n in range(2 * NT):
                    tile = q * (2 * NT) + (base + n)
                    pe.wait_ge(core.outs_free, (q * (2 * NT) + (outs + n)) * 2 + 2)
                    for i in range(RING):
                        if n == NT:
                            pe.wait_ge(f_low, q * (2 * NT) + 2 * i + 4)
                        core.multiply_slab(pe, tile, i, 2 * (n % 2), *((core.th, core.tl) if n < NT else (fh, fl)),
                                           4 * i, i == 0, i == RING - 1)
                        if i == 1 and 1 <= n <= NT:
                            turn(q, n - 1)

        @block.scalar
        def _(act):
            def read_out(q, n):
                tile = q * (2 * NT) + (base + n)
                act.wait_ge(core.slabs_used, tile * RING + (RING + 2))
                for half in range(NH):
                    nc.scalar.activation(relu[:, n % 2, half, :], core.ps[:, 2 * (n % 2) + half, :],
                                         ACT.Relu).then_inc(core.outs_free, 1)

            def high(q, n):
                for half in range(NH):
                    act.wait_ge(turned, q * (2 * NT) + 2 * n + half + 1)
                    nc.scalar.copy(fh[:, 4 * n:4 * n + 4, half * P:(half + 1) * P],
                                   core.ps[:, 4 + half, :].rearrange("p (j t) -> p j t", j=4)).then_inc(f_high, 1)

            with act.Fori(0, QUARTERS) as q:
                for n in range(2 * NT):
                    for i in range(RING):
                        core.split_high(act, q * (2 * NT) + (base + n), i)
                        if i == 0 and 1 <= n <= NT:
                            read_out(q, n - 1)
                        if i == 2 and 1 <= n <= NT:
                            high(q, n - 1)

        @block.gpsimd
        def _(pool):
            with pool.Fori(0, QUARTERS) as q:
                for n in range(NT):
                    pool.wait_ge(core.outs_free, (q * (2 * NT) + (outs + n)) * 2 + 6)
                    for half in range(NH):
                        r = relu[:, n % 2, half, :]
                        nc.gpsimd.tensor_tensor(square[:, n % 2, half, :], r, r, ALU.mult).then_inc(squared, 1)

        @block.vector
        def _(dve):
            nc.vector.memset(total[:], 0.0).then_inc(cleared, 1)
            nc.vector.memset(core.small[:, 62:63], 0.0).then_inc(f_low, 2)

            def read_out(q, n):
                tile = q * (2 * NT) + (base + NT + n)
                dve.wait_ge(core.slabs_used, tile * RING + (RING + 2))
                for half in range(NH):
                    o = total[:, half, n * 512:(n + 1) * 512]
                    nc.vector.tensor_tensor(o, core.ps[:, 2 * (n % 2) + half, :], o, ALU.add).then_inc(core.outs_free, 1)

            def low(q, n):
                for half in range(NH):
                    dve.wait_ge(f_high, q * (2 * NT) + 2 * n + half + 1)
                    o = (slice(None), slice(4 * n, 4 * n + 4), slice(half * P, (half + 1) * P))
                    nc.vector.tensor_tensor(fl[o], core.ps[:, 4 + half, :].rearrange("p (j t) -> p j t", j=4),
                                            fh[o].bitcast(F32), ALU.subtract).then_inc(f_low, 1)

            dve.wait_ge(cleared, 1)
            with dve.Fori(0, QUARTERS) as q:
                for n in range(2 * NT):
                    for i in range(RING):
                        core.split_low(dve, q * (2 * NT) + (base + n), i)
                        if i == 0 and n > NT:
                            read_out(q, n - 1 - NT)
                        if i == 2 and 1 <= n <= NT:
                            low(q, n - 1)
                read_out(q, NT - 1)
    core.tiles += QUARTERS * 2 * NT
    core.outs += QUARTERS * 2 * NT


def load_biases(sp, rpb, bias, biases_in):
    for half in range(NH):
        for r in range(P // GRID_W):
            row = half * (P // GRID_W) + r
            for k in range(ROWS):
                src = bass.AP(rpb.tensor, (WR - 1 + k - row) * (2 * WC - 1) + WC - GRID_W,
                              [[1, GRID_W], [(2 * WR - 1) * (2 * WC - 1), HEADS], [1, GRID_W]])
                dst = bias[r * GRID_W:(r + 1) * GRID_W, :, half, k * GRID_W:(k + 1) * GRID_W]
                sp.dma_start(dst, src).then_inc(biases_in, 16)


def rotate(nc, step, x1, x2, cos, sin, t1, t2):
    tt = nc.vector.tensor_tensor
    step(tt(t1, x1, sin, ALU.mult))
    step(tt(t2, x2, sin, ALU.mult))
    step(tt(x1, x1, cos, ALU.mult))
    step(tt(x2, x2, cos, ALU.mult))
    step(tt(x1, x1, t2, ALU.subtract))
    step(tt(x2, x2, t1, ALU.add))


def latent_stage(core, lat, ch, cl, kr, cos, sin, positions, scratch):
    nc = core.nc
    two_pi = 6.283185307179586
    c1 = 6.28125
    c2 = float(np.float32(two_pi - c1))
    c2 = float(np.float32(int(c2 * 2 ** 22) / 2 ** 22))
    c3 = float(np.float32(two_pi - c1 - c2))
    magic = 12582912.0
    with ExitStack() as local:
        core.local = local
        (pos_in, sums, mean_ready, rooted, done, scaled, turned, high, low, angles, tables, kr_ready, kr_turned,
         kr_read) = core.new(
            "pos_in", "sums_ready", "mean_ready", "rooted", "dve_done", "normed", "turned", "high", "low",
            "angles", "tables", "kr_ready", "kr_turned", "kr_read")
        junk, pos_i, pos, ang, turns, r_sin, r_cos, t1, t2 = core.scratch(
            scratch, ("junk", [P, 4, LORA]), ("pos_i", [P, NH], I32), ("pos", [P, NH]), ("ang", [P, NH, 32]),
            ("turns", [P, NH, 32]), ("r_sin", [P, NH, 32]), ("r_cos", [P, NH, 32]), ("t1", [P, NH, 32]),
            ("t2", [P, NH, 32]))
        ms, rf, tmp = core.small[:, 0:4], core.small[:, 4:8], core.small[:, 8:12]
        pe_part, act_part, dve_part = transpose_split(core, lat, 2 * LC, ch, cl, (turned, high, low),
                                                      lambda c: core.v("g_q_a_2", c))
        freq = core.const[:, C_FREQ:C_FREQ + 32]
        block = local.enter_context(nc.Block())

        @block.sync
        def _(sp):
            sp.dma_start(pos_i[:], positions.rearrange("b (h p) -> (b p) h", p=P),
                         allow_slow_non_contiguous=True).then_inc(pos_in, 16)

        @block.scalar
        def _(act):
            for j in range(4):
                nc.scalar.activation(junk[:, j, :], lat[:, j % 2, (j // 2) * LORA:(j // 2 + 1) * LORA], ACT.Square,
                                     accum_out=ms[:, j:j + 1]).then_inc(sums, 1)
            act.wait_ge(mean_ready, 1)
            nc.scalar.activation(tmp, ms, ACT.Sqrt).then_inc(rooted, 1)
            act_part(act)
            act.wait_ge(angles, 1)
            nc.scalar.activation(sin[:], r_sin[:], ACT.Sin).then_inc(tables, 1)
            nc.scalar.activation(cos[:], r_cos[:], ACT.Sin).then_inc(tables, 1)
            act.wait_ge(kr_turned, 1)
            nc.scalar.copy(kr[0:ROPE, :], core.ps[0:ROPE, 0, 0:T]).then_inc(kr_read, 1)

        @block.vector
        def _(dve):
            step = Steps(dve, done)
            dve.wait_ge(sums, 4)
            rms_factor(nc, dve, step, ms, rf, tmp, LORA, 1e-6, mean_ready, rooted, 1)
            for j in range(4):
                o = lat[:, j % 2, (j // 2) * LORA:(j // 2 + 1) * LORA]
                nc.vector.tensor_scalar(o, o, rf[:, j:j + 1], None, ALU.mult).then_inc(scaled, 1)
            dve_part(dve)
            dve.wait_ge(pos_in, 16)
            step(nc.vector.tensor_copy(pos[:], pos_i[:]))
            for half in range(NH):
                step(nc.vector.tensor_scalar(ang[:, half, :], freq, pos[:, half:half + 1], None, ALU.mult))
            for r, quarter in ((r_sin, 0.0), (r_cos, 0.25)):
                step(nc.vector.tensor_scalar(turns[:], ang[:], 1.0 / two_pi, quarter, ALU.mult, ALU.add))
                step(nc.vector.tensor_scalar(turns[:], turns[:], magic, None, ALU.add))
                step(nc.vector.tensor_scalar(turns[:], turns[:], magic, None, ALU.subtract))
                part = ang
                for c in (c1, c2, c3):
                    step(nc.vector.scalar_tensor_tensor(out=r[:], in0=turns[:], scalar=-c, in1=part[:],
                                                        op0=ALU.mult, op1=ALU.add))
                    part = r
                step(nc.vector.tensor_scalar(r[:], r[:], quarter * two_pi, None, ALU.add))
                ins = nc.vector.tensor_scalar(r[:], r[:], 3.1415925, -3.1415925, ALU.min, ALU.max)
                if quarter:
                    ins.then_inc(angles, 1)
                else:
                    step(ins)
            dve.wait_ge(tables, 2)
            k = lat[:, :, 2 * LORA:]
            rotate(nc, step, k[:, :, 0:32], k[:, :, 32:64], cos[:], sin[:], t1[:], t2[:])
            nc.vector.memset(core.small[:, 62:63], 0.0).then_inc(kr_ready, 1)

        @block.tensor
        def _(pe):
            pe.wait_ge(scaled, 4)
            pe_part(pe)
            pe.wait_ge(kr_ready, 1)
            for half in range(NH):
                last = nc.tensor.transpose(core.ps[0:ROPE, 0, half * P:(half + 1) * P],
                                           lat[:, half, 2 * LORA:], core.ident)
            last.then_inc(kr_turned, 1)


UQ_W = 384


def latent_sources(w_uq, w_ukv):
    uq = w_uq.rearrange("(c p) h k -> p c (h k)", p=P)
    ukv = w_ukv.rearrange("(c p) h k -> p c (h k)", p=P)

    def source(u):
        if u < 2:
            return lambda i: uq[:, :, (4 * u + i) * UQ_W:(4 * u + i + 1) * UQ_W]
        return lambda i: ukv[:, :, (4 * u + i - 8) * 512:(4 * u + i - 7) * 512]

    return source


def latent_dense(core, source, ch, cl, q, kv, nexts):
    nc, base, outs = core.nc, core.tiles, core.outs
    with nc.Block() as block:

        def width(s):
            return UQ_W if s < 8 else 512

        @block.sync
        def _(sp):
            for u in range(1, 4):
                for i in range(RING):
                    core.load_slab(sp, source(u), base + u, i)
            for i in range(RING):
                core.load_slab(sp, nexts, base + 4, i)

        @block.tensor
        def _(pe):
            for part in range(2):
                with pe.Fori(0, 2) as u:
                    for i in range(RING):
                        tile = u + (base + 2 * part)
                        pe.wait_ge(core.outs_free, u * 8 + (outs + 8 * part + i) * 2 + 2)
                        core.multiply_slab(pe, tile, i, 2 * (i % 2), ch, cl, LC * part, True, True, width(8 * part))

        @block.scalar
        def _(act):
            def read_out(s):
                act.wait_ge(core.slabs_used, base * RING + s + 3)
                w = width(s)
                o = q[:, :, s * w:(s + 1) * w] if s < 8 else kv[:, :, (s - 8) * w:(s - 7) * w]
                for half in range(NH):
                    nc.scalar.copy(o[:, half], core.ps[:, 2 * (s % 2) + half, 0:w]).then_inc(core.outs_free, 1)

            for s in range(16):
                core.split_high(act, base + s // RING, s % RING, width(s))
                if s:
                    read_out(s - 1)
            read_out(15)

        @block.vector
        def _(dve):
            for s in range(16):
                core.split_low(dve, base + s // RING, s % RING, width(s))

    core.tiles += 4
    core.outs += 16


def rotate_stage(core, q, cos, sin, scratch):
    nc = core.nc
    with ExitStack() as local:
        core.local = local
        done, = core.new("dve_done")
        t1, t2 = core.scratch(scratch, ("t1", [P, HEADS, 32]), ("t2", [P, HEADS, 32]))
        block = local.enter_context(nc.Block())

        @block.vector
        def _(dve):
            step = Steps(dve, done)
            for half in range(NH):
                heads = q[:, half, :].rearrange("p (h k) -> p h k", k=QK)
                c, s = (t[:, half, :].unsqueeze(1).broadcast_to([P, HEADS, 32]) for t in (cos, sin))
                rotate(nc, step, heads[:, :, NOPE:NOPE + 32], heads[:, :, NOPE + 32:], c, s, t1[:], t2[:])


def sgu_stage(core, z, w_spatial, ln_g, ln_b, scratch):
    nc = core.nc
    with ExitStack() as local:
        core.local = local
        (w_in, g_in, b_in, turned, w_ready, sums, centred, mean_ready, rooted, done, normed, mixed, read) = core.new(
            "w_in", "g_in", "b_in", "turned", "w_ready", "sums", "centred", "mean_ready", "rooted", "dve_done",
            "normed", "mixed", "read")
        w, wt, g_rows, b_rows, junk = core.scratch(
            scratch, ("w_spatial", [P, GROUPS, P]), ("w_spatial_t", [P, GROUPS, P]), ("ln_g_rows", [P, D]),
            ("ln_b_rows", [P, D]), ("junk", [P, D]))
        mean, ms, rf, tmp = (core.small[:, k:k + 2] for k in (0, 2, 4, 6))
        tril = core.const[:, C_TRIL:C_TRIL + P]
        u, v = z[:, :, :D], z[:, :, D:]
        block = local.enter_context(nc.Block())

        @block.sync
        def _(sp):
            sp.dma_start(w[:], w_spatial.rearrange("g t s -> t g s")).then_inc(w_in, 16)
            sp.dma_start(g_rows[:], ln_g.partition_broadcast(P)).then_inc(g_in, 16)
            sp.dma_start(b_rows[:], ln_b.partition_broadcast(P)).then_inc(b_in, 16)

        @block.tensor
        def _(pe):
            pe.wait_ge(w_in, 16)
            for g in range(GROUPS):
                last = nc.tensor.transpose(core.ps[:, g // 4, (g % 4) * P:(g % 4 + 1) * P], w[:, g, :], core.ident)
            last.then_inc(turned, 1)
            pe.wait_ge(w_ready, 2)
            pe.wait_ge(normed, NH)
            for g in range(GROUPS):
                if g >= 4:
                    pe.wait_ge(read, 2 * (g - 3))
                for half in range(NH):
                    last = nc.tensor.matmul(core.ps[:, 4 + g % 4, half * GD:(half + 1) * GD], wt[:, g, :],
                                            v[:, half, g * GD:(g + 1) * GD], start=True, stop=True)
                last.then_inc(mixed, 1)

        @block.scalar
        def _(act):
            for half in range(NH):
                if half:
                    act.wait_ge(sums, half)
                nc.scalar.activation(junk[:], v[:, half, :], ACT.Identity,
                                     accum_out=mean[:, half:half + 1]).then_inc(sums, 1)
            for half in range(NH):
                act.wait_ge(centred, half + 1)
                act.wait_ge(sums, 2 + half)
                nc.scalar.activation(junk[:], v[:, half, :], ACT.Square,
                                     accum_out=ms[:, half:half + 1]).then_inc(sums, 1)
            act.wait_ge(mean_ready, 1)
            nc.scalar.activation(tmp, ms, ACT.Sqrt).then_inc(rooted, 1)

        @block.vector
        def _(dve):
            step = Steps(dve, done)
            dve.wait_ge(turned, 1)
            for b in range(2):
                nc.vector.tensor_tensor(wt[:, 4 * b:4 * b + 4, :], core.ps[:, b, :].rearrange("p (g t) -> p g t", g=4),
                                        tril.unsqueeze(1).broadcast_to([P, 4, P]), ALU.mult).then_inc(w_ready, 1)
            dve.wait_ge(sums, 2)
            step(nc.vector.tensor_scalar(mean, mean, 1.0 / D, None, ALU.mult))
            for half in range(NH):
                nc.vector.tensor_scalar(v[:, half, :], v[:, half, :], mean[:, half:half + 1], None,
                                        ALU.subtract).then_inc(centred, 1)
            dve.wait_ge(sums, 4)
            rms_factor(nc, dve, step, ms, rf, tmp, D, 1e-6, mean_ready, rooted, 1)
            dve.wait_ge(g_in, 16)
            dve.wait_ge(b_in, 16)
            for half in range(NH):
                step(nc.vector.scalar_tensor_tensor(out=v[:, half, :], in0=v[:, half, :], scalar=rf[:, half:half + 1],
                                                    in1=g_rows[:], op0=ALU.mult, op1=ALU.mult))
                nc.vector.tensor_tensor(v[:, half, :], v[:, half, :], b_rows[:], ALU.add).then_inc(normed, 1)
            for g in range(GROUPS):
                dve.wait_ge(mixed, g + 1)
                for half in range(NH):
                    o = u[:, half, g * GD:(g + 1) * GD]
                    nc.vector.scalar_tensor_tensor(out=o, in0=core.ps[:, 4 + g % 4, half * GD:(half + 1) * GD],
                                                   scalar=core.v("b_spatial_2", g), in1=o, op0=ALU.add,
                                                   op1=ALU.mult).then_inc(read, 1)


def merge_stage(core, gates, b_gate, oa, z):
    nc = core.nc
    with ExitStack() as local:
        core.local = local
        b_in, biased, opened, done, merged, turned, high, low = core.new(
            "b_in", "biased", "opened", "dve_done", "merged", "turned", "high", "low")
        rows = z[:, :, D:]
        pe_part, act_part, dve_part = transpose_split(core, oa, DC, core.th, core.tl, (turned, high, low))
        block = local.enter_context(nc.Block())

        @block.sync
        def _(sp):
            for j in range(2):
                sp.dma_start(rows[:, j, :], b_gate[j * D:(j + 1) * D].partition_broadcast(P)).then_inc(b_in, 16)

        @block.scalar
        def _(act):
            for n in range(4):
                act.wait_ge(biased, n + 1)
                g = gates[:, n // 2, (n % 2) * D:(n % 2 + 1) * D]
                nc.scalar.activation(g, g, ACT.Sigmoid).then_inc(opened, 1)
            act_part(act)

        @block.vector
        def _(dve):
            step = Steps(dve, done)
            dve.wait_ge(b_in, 32)
            for n in range(4):
                g = gates[:, n // 2, (n % 2) * D:(n % 2 + 1) * D]
                nc.vector.tensor_tensor(g, g, rows[:, n % 2, :], ALU.add).then_inc(biased, 1)
            for half in range(NH):
                dve.wait_ge(opened, 2 * half + 2)
                step(nc.vector.tensor_tensor(oa[:, half, :], oa[:, half, :], gates[:, half, :D], ALU.mult))
                step(nc.vector.tensor_tensor(z[:, half, :D], z[:, half, :D], gates[:, half, D:], ALU.mult))
                nc.vector.tensor_tensor(oa[:, half, :], oa[:, half, :], z[:, half, :D], ALU.add).then_inc(merged, 1)
            dve_part(dve)

        @block.tensor
        def _(pe):
            pe.wait_ge(merged, NH)
            pe_part(pe)


def key_stage(core, pq_t, keys, keys_t, peer_keys, sub):
    nc = core.nc
    sets = 2 * PH
    with ExitStack() as local:
        core.local = local
        keys_in, turned, copied, scored, read = core.new("keys_in", "turned", "copied", "scored", "read")
        block = local.enter_context(nc.Block())

        @block.sync
        def _(sp):
            sp.dma_start(keys[:], peer_keys.rearrange("h s n k -> n (h s) k")).then_inc(keys_in, 16)

        @block.tensor
        def _(pe):
            pe.wait_ge(keys_in, 16)
            for b in range(4):
                for j in range(4):
                    last = nc.tensor.transpose(core.ps[:, b, j * P:(j + 1) * P], keys[:, 4 * b + j, :], core.ident)
                last.then_inc(turned, 1)
            for half in range(NH):
                for b in range(4):
                    if half:
                        pe.wait_ge(read, b + 1)
                    else:
                        pe.wait_ge(copied, b + 1)
                    for j in range(4):
                        s = 4 * b + j
                        last = nc.tensor.matmul(core.ps[:, 4 + b, j * P:(j + 1) * P], pq_t[:, s, half * P:(half + 1) * P],
                                                keys_t[:, s, :], start=True, stop=True)
                    last.then_inc(scored, 1)

        @block.scalar
        def _(act):
            for b in range(4):
                act.wait_ge(turned, b + 1)
                nc.scalar.copy(keys_t[:, 4 * b:4 * b + 4, :], core.ps[:, b, :].rearrange("p (j n) -> p j n", j=4)).then_inc(copied, 1)

        @block.vector
        def _(dve):
            for n in range(8):
                half, b = n // 4, n % 4
                dve.wait_ge(scored, n + 1)
                nc.vector.tensor_copy(sub[:, half, 4 * b:4 * b + 4, :],
                                      core.ps[:, 4 + b, :].rearrange("p (j n) -> p j n", j=4)).then_inc(read, 1)


def pick_stage(core, sub, gate, index, scratch):
    nc = core.nc
    K2 = TOPK * TOPK
    with ExitStack() as local:
        core.local = local
        done, shifted, exped = core.new("dve_done", "shifted", "exponentiated")
        best, at, cand, pos, best_f, row, col, top, one, total = core.scratch(
            scratch, ("best", [P, NH, 2 * PH, TOPK]), ("best_at", [P, NH, 2 * PH, TOPK], U32),
            ("cand", [P, PH, K2]), ("cand_at", [P, NH, PH, TOPK], U32),
            ("best_at_f", [P, NH, 2 * PH, TOPK]), ("cand_row", [P, NH, PH, TOPK]), ("cand_col", [P, NH, PH, TOPK]),
            ("top", [P, NH, PH, TOPK]), ("one_hot", [P, PH, TOPK, TOPK]), ("total", [P, NH * PH]))
        block = local.enter_context(nc.Block())
        iota = core.const[:, C_IOTA:C_IOTA + TOPK].unsqueeze(1).broadcast_to([P, TOPK, TOPK])
        every = "p a b k -> p (a b) k"

        def sixteen(step, values, out, where):
            for r in range(2):
                o, w = out[:, 8 * r:8 * r + 8], where[:, 8 * r:8 * r + 8]
                step(nc.vector.max(o, values))
                step(nc.vector.max_index(w, o, values))
                if r == 0:
                    step(nc.vector.match_replace(values, o, values, -3e38))

        @block.vector
        def _(dve):
            step = Steps(dve, done)
            for half in range(NH):
                for s in range(2 * PH):
                    sixteen(step, sub[:, half, s, :], best[:, half, s, :], at[:, half, s, :])
            step(nc.vector.tensor_copy(best_f[:], at[:]))
            for half in range(NH):
                for h in range(PH):
                    step(nc.vector.tensor_tensor(
                        cand[:, h, :].rearrange("p (a b) -> p a b", a=TOPK),
                        best[:, half, 2 * h, :].unsqueeze(2).broadcast_to([P, TOPK, TOPK]),
                        best[:, half, 2 * h + 1, :].unsqueeze(1).broadcast_to([P, TOPK, TOPK]), ALU.add))
                for h in range(PH):
                    sixteen(step, cand[:, h, :], top[:, half, h, :], pos[:, half, h, :])
            groups = top[:].rearrange(every)
            step(nc.vector.tensor_reduce(total[:], groups, AX.X, ALU.max))
            nc.vector.tensor_tensor(groups, groups, total[:].unsqueeze(2).broadcast_to([P, NH * PH, TOPK]),
                                    ALU.subtract).then_inc(shifted, 1)
            row_u, col_u = (t[:].bitcast(U32) for t in (row, col))
            step(nc.vector.tensor_scalar(row_u, pos[:], 4, None, ALU.logical_shift_right))
            step(nc.vector.tensor_scalar(col_u, pos[:], 15, None, ALU.bitwise_and))
            step(nc.vector.tensor_copy(row[:], row_u))
            step(nc.vector.tensor_copy(col[:], col_u))
            for half in range(NH):
                for s, which in enumerate((row, col)):
                    for h in range(PH):
                        step(nc.vector.tensor_tensor(one[:, h], iota, which[:, half, h, :].unsqueeze(2).broadcast_to([P, TOPK, TOPK]),
                                                     ALU.is_equal))
                        step(nc.vector.tensor_tensor(one[:, h], one[:, h],
                                                     best_f[:, half, 2 * h + s, :].unsqueeze(1).broadcast_to([P, TOPK, TOPK]),
                                                     ALU.mult))
                    step(nc.vector.tensor_reduce(which[:, half].rearrange("p h k -> p (h k)"),
                                                 one[:].rearrange("p h a b -> p (h a) b"), AX.X, ALU.add))
            step(nc.vector.scalar_tensor_tensor(out=row[:], in0=row[:], scalar=float(NKEYS), in1=col[:],
                                                op0=ALU.mult, op1=ALU.add))
            step(nc.vector.tensor_copy(index[:], row[:].rearrange("p a b k -> p (a b k)")))
            dve.wait_ge(exped, 1)
            step(nc.vector.tensor_reduce(total[:], groups, AX.X, ALU.add))
            step(nc.vector.reciprocal(total[:], total[:]))
            step(nc.vector.tensor_tensor(gate[:].rearrange("p (g k) -> p g k", k=TOPK), groups,
                                         total[:].unsqueeze(2).broadcast_to([P, NH * PH, TOPK]), ALU.mult))

        @block.scalar
        def _(act):
            act.wait_ge(shifted, 1)
            nc.scalar.activation(top[:], top[:], ACT.Exp).then_inc(exped, 1)


def expert_stage(core, h2, index, gate, peer_u, peer_v, acc, scratch):
    nc = core.nc
    rounds = PICKS // GR
    with ExitStack() as local:
        core.local = local
        primed, staged, freed, dots_kept, gelued, weighted, staged_w, cleared = core.new(
            "primed", "index_staged", "rows_used", "dots_kept", "gelued", "weighted", "weights_staged", "cleared")
        landed = core.new(*[f"row_landed{i}" for i in range(GR)])
        rows, junk, slot, dot, keep, weights, carrier = core.scratch(
            scratch, ("expert_rows", [P, GR, D]), ("junk", [P, D]), ("index_slots", [P, GR], U32),
            ("dot_slots", [P, GR]), ("dots", [P, NH * PICKS]), ("weight_slots", [P, GR]),
            ("carrier", [P, 2]))
        block = local.enter_context(nc.Block())

        @block.gpsimd
        def _(pool):
            nc.gpsimd.memset(carrier[:, 0:1], 0.0).then_inc(primed, 1)
            pool.wait_ge(primed, 1)
            for half in range(NH):
                for part, table in enumerate((peer_u, peer_v)):
                    at = (2 * half + part) * PICKS
                    with pool.Fori(0, rounds) as r:
                        for i in range(GR):
                            pool.wait_ge(freed, r * GR + (at + i + 1))
                            nc.gpsimd.tensor_copy(slot[:, i:i + 1], index[:, bass.ds(r * GR + (half * PICKS + i), 1)]
                                                  ).then_inc(staged, 1)
                            pool.wait_ge(staged, r * GR + (at + i + 1))
                            nc.gpsimd.tensor_tensor(carrier[:, 1:2], carrier[:, 0:1], carrier[:, 0:1], ALU.mult)
                            nc.gpsimd.indirect_dma_start(
                                rows[:, i, :], None, table, bass.IndirectOffsetOnAxis(ap=slot[:, i:i + 1], axis=0)
                            ).then_inc(landed[i], 16)

        @block.vector
        def _(dve):
            nc.vector.memset(acc[:], 0.0).then_inc(cleared, 1)
            dve.wait_ge(cleared, 1)
            nc.vector.memset(dot[:], 0.0).then_inc(freed, GR)
            for half in range(NH):
                at = 2 * half * PICKS
                with dve.Fori(0, rounds) as r:
                    for i in range(GR):
                        dve.wait_ge(landed[i], r * 16 + (at // GR * 16 + 16))
                        dve.wait_ge(freed, r * GR + (at + i + GR))
                        nc.vector.tensor_tensor_reduce(out=junk[:], in0=rows[:, i, :], in1=h2[:, half, :], scale=1.0,
                                                       scalar=0.0, op0=ALU.mult, op1=ALU.add,
                                                       accum_out=dot[:, i:i + 1]).then_inc(freed, 1)
                    dve.wait_ge(freed, r * GR + (at + 2 * GR))
                    nc.vector.tensor_copy(keep[:, bass.ds(r * GR + half * PICKS, GR)], dot[:]).then_inc(dots_kept, 1)
                    dve.wait_ge(dots_kept, r + (half * rounds + 1))
                dve.wait_ge(gelued, half + 1)
                mine = keep[:, half * PICKS:(half + 1) * PICKS]
                nc.vector.tensor_tensor(mine, mine, gate[:, half * PICKS:(half + 1) * PICKS], ALU.mult).then_inc(weighted, 1)
                dve.wait_ge(weighted, half + 1)
                at = (2 * half + 1) * PICKS
                with dve.Fori(0, rounds) as r:
                    dve.wait_ge(freed, r * GR + (at + GR))
                    nc.vector.tensor_copy(weights[:], keep[:, bass.ds(r * GR + half * PICKS, GR)]).then_inc(staged_w, 1)
                    dve.wait_ge(staged_w, r + (half * rounds + 1))
                    for i in range(GR):
                        dve.wait_ge(landed[i], r * 16 + (at // GR * 16 + 16))
                        dve.wait_ge(freed, r * GR + (at + i + GR))
                        nc.vector.scalar_tensor_tensor(out=acc[:, half, :], in0=rows[:, i, :], scalar=weights[:, i:i + 1],
                                                       in1=acc[:, half, :], op0=ALU.mult, op1=ALU.add).then_inc(freed, 1)
                dve.wait_ge(freed, at + PICKS + GR)

        @block.scalar
        def _(act):
            for half in range(NH):
                act.wait_ge(dots_kept, (half + 1) * rounds)
                mine = keep[:, half * PICKS:(half + 1) * PICKS]
                nc.scalar.activation(mine, mine, ACT.Gelu_apprx_tanh).then_inc(gelued, 1)


def build(nc, ins, out):
    with ExitStack() as ctx:
        core = Core(nc, ctx)
        KB = 1024
        place = core.place
        w_in, w_out, w_up, w_down = (ins[n][0] for n in ("w_in", "w_out", "w_up", "w_down"))
        w_in2, w_out2 = ins["w_in_2"][0], ins["w_out_2"][0]
        w_peer_q = ins["w_peer_q_2"][0].rearrange("d h k -> d (h k)")

        normed = place("normed", [P, NH, D], at=0)
        setup_stage(core, ins, tile_view(w_in, 0))
        norm_stage(core, None, 1e-6, normed, 16 * KB, gain_name="pre_mix_g")

        glu = place("a_and_gate", [P, NH, D], at=0)
        ut = place("gated_turned", [P, CC, PADT], at=16 * KB)
        conv = place("conv", [P, CC, T], at=26 * KB)
        qkv = place("qkv", [P, NH, 3 * CW], at=37152)
        bias = place("biases", [P, HEADS, NH, T], at=61728)

        def copy_to(dst):
            def evacuate(act, t, half, psum):
                return nc.scalar.copy(dst[:, half, bass.ds(t * 512, psum.shape[-1])], psum)
            return evacuate

        dense(core, "a_gate", 4, lambda t: tile_view(w_in, t * 512), copy_to(glu), tile_view(w_in, 2 * CW))
        gated_stage(core, glu, ut)
        wdw = place("w_dw_rows", [TAPS, CW], at=0)
        wdw_t = place("w_dw_turned", [P, CC, 32], at=4 * KB)
        turn_taps_stage(core, ins["w_dw"][0], wdw, wdw_t)

        with ExitStack() as local:
            core.local = local
            taps, biases_in = core.new("taps_done", "biases_in")
            count = [0]

            def convolve(dve, slab):
                c, third = slab // 3, slab % 3
                for k in range((0, 11, 21)[third], (11, 21, 31)[third]):
                    if count[0]:
                        dve.wait_ge(taps, count[0])
                    u, w = ut[:, c, k:k + T], wdw_t[:, c, k:k + 1]
                    if k == 0:
                        ins_ = nc.vector.tensor_scalar(conv[:, c, :], u, w, core.v("b_dw", c), ALU.mult, ALU.add)
                    else:
                        ins_ = nc.vector.scalar_tensor_tensor(out=conv[:, c, :], in0=u, scalar=w, in1=conv[:, c, :],
                                                              op0=ALU.mult, op1=ALU.add)
                    ins_.then_inc(taps, 1)
                    count[0] += 1

            dense(core, "qkv", 6, lambda t: tile_view(w_in, t * 512 + 2 * CW), copy_to(qkv),
                  tile_view(w_out, 0), dve_slab=convolve, 
                  before=lambda sp: load_biases(sp, ins["rpb"][0], bias, biases_in))

        xc = place("centred", [P, CC, T], at=0)
        sq = place("squares", [P, CC, T], at=8 * KB)
        stat = place("stats", [P, 3, T], at=16 * KB)
        conv_norm_stage(core, conv, xc, sq, stat, 19 * KB)

        q_t = place("q_turned", [P, CC, T], at=0)
        k_t = place("k_turned", [P, CC, T], at=8 * KB)
        attended = place("attended", [P, NH, CW], at=16 * KB)
        turn_stage(core, qkv, 2 * CC, lambda c: (q_t if c < CC else k_t)[:, c % CC, :])

        def na_products(h, half, n):
            at = (h % 2) * HD
            return [(q_t[at:at + HD, h // 2, half * P:(half + 1) * P], k_t[at:at + HD, h // 2, 0:n])]

        def mask_biases(pool, ready):
            pool.wait_ge(biases_in, 16 * ROWS * T // GRID_W)
            window = core.const[:, C_NA:C_NA + T].unsqueeze(1).broadcast_to([P, HEADS * NH, T])
            every = bias[:].rearrange("p h a t -> p (h a) t")
            nc.gpsimd.tensor_tensor(every, every, window, ALU.add).then_inc(ready, 1)

        def head_biases(h):
            b = bias[:, h]
            return bass.AP(b.tensor, b.offset + GRID_W - 1, [list(b.ap[0]), [GRID_W, NH * ROWS], [-1, GRID_W]])

        attention_stage(core, HEADS, HD ** -0.5, ((0, T), (T, T)), head_biases, na_products,
                        lambda h, k: qkv[:, k, 2 * CW + h * HD:2 * CW + (h + 1) * HD], HD, attended, 24 * KB,
                        prepare=mask_biases)
        split_stage(core, attended, CC, core.th[:, CC:, :], core.tl[:, CC:, :])

        mix = place("mix", [P, NH, D], at=0)
        normed = place("normed_2", [P, NH, D], at=16 * KB)
        dense(core, "w_out", 4, lambda t: tile_view(w_out, t * 512), copy_to(mix), tile_view(w_up, 0))
        norm_stage(core, mix, 1e-6, normed, 32 * KB, post_gain=ins["post_mix_g"][0], post_eps=1e-6,
                   gain_name="pre_mlp_g")

        mlp = place("mlp", [P, NH, D], at=48 * KB)
        mlp_stage(core, w_up, w_down, mlp, tile_view(w_in2, 0), 0)
        normed = place("normed_3", [P, NH, D], at=0)
        norm_stage(core, mlp, 1e-6, normed, 16 * KB, post_gain=ins["post_mlp_g"][0], post_eps=1e-6,
                   gain_name="g_norm1_2")

        KPE, Z0 = 2 * LORA, 2 * LORA + ROPE
        lat = place("latents", [P, NH, 2 * LORA + ROPE], at=16 * KB)
        ch = place("latent_high", [P, 2 * LC, T], F32R, at=0)
        cl = place("latent_low", [P, 2 * LC, T], F32R, at=8 * KB)
        kr = place("rotated_key", [P, T], at=88 * KB)
        cos = place("cos", [P, NH, 32], at=89 * KB)
        sin = place("sin", [P, NH, 32], at=89 * KB + 256)
        source = latent_sources(ins["w_uq_2"][0], ins["w_ukv_2"][0])
        dense(core, "latents", 2, lambda t: tile_view(w_in2, t * 512), copy_to(lat), tile_view(w_in2, KPE, ROPE))

        def copy_kpe(act, t, half, psum):
            return nc.scalar.copy(lat[:, half, KPE:], psum)

        dense(core, "shared_key", 1, None, copy_kpe, source(0), w=ROPE)
        latent_stage(core, lat, ch, cl, kr, cos, sin, ins["positions_2"], 40 * KB)
        q = place("q", [P, NH, HEADS * QK], at=16 * KB)
        kv = place("kv", [P, NH, HEADS * 2 * NOPE], at=40 * KB)
        latent_dense(core, source, ch, cl, q, kv, tile_view(w_in2, Z0))
        rotate_stage(core, q, cos, sin, 72 * KB)

        oa = place("latent_attended", [P, NH, D], at=0)
        qk_t = place("head_qk_turned", [P, 2, 2 * T], at=72 * KB)
        qr_t = place("head_rotary_turned", [P, 2, T], at=76 * KB)

        def mla_turn(h):
            moves = []
            for half in range(NH):
                cols = slice(half * P, (half + 1) * P)
                moves.append((core.ps[:, 6, cols], q[:, half, h * QK:h * QK + NOPE]))
                moves.append((core.ps[:, 6, T + half * P:T + (half + 1) * P], kv[:, half, h * 2 * NOPE:(2 * h + 1) * NOPE]))
                moves.append((core.ps[0:ROPE, 7, cols], q[:, half, h * QK + NOPE:(h + 1) * QK]))
            return moves, (qk_t[:, h % 2, :], core.ps[:, 6, :]), (qr_t[0:ROPE, h % 2, :], core.ps[0:ROPE, 7, 0:T])

        def mla_products(h, half, n):
            cols = slice(half * P, (half + 1) * P)
            return [(qk_t[:, h % 2, cols], qk_t[:, h % 2, T:T + n]), (qr_t[0:ROPE, h % 2, cols], kr[0:ROPE, 0:n])]

        causal3 = place("causal_masks", [P, 3 * P], at=90 * KB)
        causal_mask_stage(core, causal3)
        attention_stage(core, HEADS, QK ** -0.5, ((0, P), (P, T)), lambda h: causal3[:], mla_products,
                        lambda h, k: kv[:, k, (2 * h + 1) * NOPE:(2 * h + 2) * NOPE], VH, oa, 78 * KB, turn=mla_turn)

        core.clear_semaphores()
        z = place("z", [P, NH, 2 * D], at=16 * KB)

        def gelu_to(act, t, half, psum):
            return nc.scalar.activation(z[:, half, bass.ds(t * 512, 512)], psum, ACT.Gelu_apprx_tanh)

        dense(core, "z", 8, lambda t: tile_view(w_in2, t * 512 + Z0), gelu_to, tile_view(w_in2, Z0 + 2 * D))
        sgu_stage(core, z, ins["w_spatial_2"][0], ins["sgu_ln_g_2"][0], ins["sgu_ln_b_2"][0], 48 * KB)
        gates = place("gates", [P, NH, 2 * D], at=48 * KB)
        dense(core, "gates", 8, lambda t: tile_view(w_in2, t * 512 + (Z0 + 2 * D)), copy_to(gates),
              tile_view(w_out2, 0))
        merge_stage(core, gates, ins["b_gate_2"][0], oa, z)
        y = place("merged_out", [P, NH, D], at=16 * KB)
        dense(core, "w_out_2", 4, lambda t: tile_view(w_out2, t * 512), copy_to(y), tile_view(w_peer_q, 0))

        h2 = place("h2", [P, NH, D], at=0)
        norm_stage(core, y, 1e-6, h2, 32 * KB, token_gain=ins["g_norm2_2"][0])
        pq = place("peer_queries", [P, NH, D], at=32 * KB)
        dense(core, "w_peer_q", 4, lambda t: tile_view(w_peer_q, t * 512), copy_to(pq), None)
        pq_t = place("peer_queries_turned", [P, DC, T], at=48 * KB)
        turn_stage(core, pq, DC, lambda c: pq_t[:, c, :])
        keys = place("keys", [P, 2 * PH, P], at=64 * KB)
        keys_t = place("keys_turned", [P, 2 * PH, P], at=72 * KB)
        sub = place("key_scores", [P, NH, 2 * PH, NKEYS], at=16 * KB)
        key_stage(core, pq_t, keys, keys_t, ins["peer_keys_2"][0], sub)
        gate = place("gate", [P, NH * PICKS], at=90 * KB)
        index = place("index", [P, NH * PICKS], U32, at=91 * KB)
        pick_stage(core, sub, gate, index, 32 * KB)
        acc = core.ring[:].rearrange("p r c n -> p (r c n)")[:, 0:NH * D].rearrange("p (h d) -> p h d", h=NH)
        expert_stage(core, h2, index, gate, ins["peer_u_2"][0], ins["peer_v_2"][0], acc, 16 * KB)
        last = place("result", [P, NH, D], at=0)
        norm_stage(core, acc, 1e-6, last, 16 * KB, token_gain=ins["g_final_2"], out=out[0])


def turn_taps_stage(core, w_dw, rows, turned_taps):
    nc = core.nc
    with ExitStack() as local:
        core.local = local
        taps_in, turned, copied = core.new("taps_in", "turned", "copied")
        block = local.enter_context(nc.Block())

        @block.sync
        def _(sp):
            sp.dma_start(rows[:], w_dw).then_inc(taps_in, 16)

        @block.tensor
        def _(pe):
            pe.wait_ge(taps_in, 16)
            for c in range(CC):
                last = nc.tensor.transpose(core.ps[:, 4, c * 32:c * 32 + TAPS], rows[:, c * P:(c + 1) * P],
                                           core.ident[0:TAPS, 0:TAPS])
            last.then_inc(turned, 1)

        @block.vector
        def _(dve):
            dve.wait_ge(turned, 1)
            nc.vector.tensor_copy(turned_taps[:, :, 0:TAPS],
                                  core.ps[:, 4, 0:CC * 32].rearrange("p (c k) -> p c k", k=32)[:, :, 0:TAPS]).then_inc(copied, 1)


def causal_mask_stage(core, masks):
    nc = core.nc
    with ExitStack() as local:
        core.local = local
        made, = core.new("masks_made")
        block = local.enter_context(nc.Block())

        @block.gpsimd
        def _(pool):
            nc.gpsimd.memset(masks[:, P:2 * P], 0.0).then_inc(made, 1)
            for b in (0, 2):
                nc.gpsimd.tensor_copy(masks[:, b * P:(b + 1) * P], core.const[:, C_CAUSAL:C_CAUSAL + P]).then_inc(made, 1)


_INS = ["x", "w_in", "w_dw", "b_dw", "conv_ln_g", "conv_ln_b", "rpb", "w_out", "w_up", "w_down", "pre_mix_g",
        "post_mix_g", "pre_mlp_g", "post_mlp_g", "positions_2", "g_norm1_2", "w_in_2", "g_q_a_2", "w_uq_2",
        "g_kv_a_2", "w_ukv_2", "sgu_ln_g_2", "sgu_ln_b_2", "w_spatial_2", "b_spatial_2", "b_gate_2", "w_out_2",
        "g_norm2_2", "w_peer_q_2", "peer_keys_2", "peer_u_2", "peer_v_2", "g_final_2"]


def kernel(**inputs):
    import numpy as _np
    import concourse.bacc as _bacc
    from concourse import mybir as _mybir
    from concourse.bass_utils import run_bass_kernel_spmd as _run

    nc = _bacc.Bacc("TRN2", target_bir_lowering=False, num_devices=1)
    arrays, ins = {}, {}
    for name in _INS:
        a = _np.asarray(inputs[name])
        if name == "rpb":
            a = a[..., ::-1]
        a = _np.ascontiguousarray(a)
        arrays[f"in_{name}"] = a
        ins[name] = nc.dram_tensor(f"in_{name}", a.shape, _mybir.dt.from_np(a.dtype), kind="ExternalInput").ap()
    arrays["shape_constants"] = shape_constants()
    ins["shape_constants"] = nc.dram_tensor("shape_constants", (P, C_ALL), F32, kind="ExternalInput").ap()
    for name in ("peer_u_2", "peer_v_2"):
        assert ins[name].shape[0] == 1
    out = nc.dram_tensor("out", (1, T, D), F32, kind="ExternalOutput").ap()
    build(nc, ins, out)
    r = _run(nc, [arrays], core_ids=[0])
    return r.results[0]["out"]
```

```python
from contextlib import ExitStack

import concourse.bass as bass
import numpy as np
from concourse import mybir

F32 = mybir.dt.float32
F32R = mybir.dt.float32r
I32 = mybir.dt.int32
U32 = mybir.dt.uint32
ACT = mybir.ActivationFunctionType
ALU = mybir.AluOpType
AX = mybir.AxisListType

P = 128
T = 256
NH = T // P
D = 2048
DC = D // P
CW = D // 2
CC = CW // P
TAPS = 31
PADT = T + TAPS - 1
HEADS, HD = 16, 64
GRID_W, WR, WC = 64, 8, 16
ROWS = T // GRID_W
FF = 4 * D
QUARTERS = FF // D
LORA, NOPE, ROPE, VH = 512, 128, 64, 128
QK = NOPE + ROPE
LC = LORA // P
GROUPS, GD = 8, 256
PH, NKEYS, TOPK = 8, 128, 16
PICKS = PH * TOPK
RING = 4
KPE_W = 256
GR = 8
NEG = -1e30

C_ID, C_NA, C_CAUSAL, C_TRIL, C_FREQ, C_IOTA = 0, 128, 384, 512, 640, 672
C_KEPT = 688
C_ALL = 800

VECS = [("pre_mix_g", DC), ("pre_mlp_g", DC), ("g_norm1_2", DC), ("g_norm2_2", DC), ("conv_ln_g", CC),
        ("conv_ln_b", CC), ("b_dw", CC), ("g_q_a_2", LC), ("g_kv_a_2", LC), ("b_spatial_2", GROUPS)]
VEC_AT = {}
_at = 0
for _name, _n in VECS:
    VEC_AT[_name] = _at
    _at += _n
VEC_ROWS = _at


def shape_constants():
    c = np.zeros((P, C_ALL), np.float32)
    i, j = np.arange(P)[:, None], np.arange(P)[None, :]
    c[:, C_ID:C_ID + P] = i == j
    col, key = np.arange(P)[:, None] % GRID_W, np.arange(T)[None, :] % GRID_W
    start = np.clip(col - WC // 2, 0, GRID_W - WC)
    window = np.where((key >= start) & (key < start + WC), 0.0, NEG)
    c[:, C_NA:C_NA + T] = window.reshape(P, ROWS, GRID_W)[:, :, ::-1].reshape(P, T)
    c[:, C_CAUSAL:C_CAUSAL + P] = np.where(j <= i, 0.0, NEG)
    c[:, C_TRIL:C_TRIL + P] = i <= j
    half = ROPE // 2
    c[:, C_FREQ:C_FREQ + half] = 10000.0 ** (-np.arange(0, ROPE, 2) / ROPE)
    c[:, C_IOTA:C_IOTA + NKEYS] = np.arange(NKEYS)
    return c


class Steps:

    def __init__(self, eng, sem, start=0):
        self.eng, self.sem, self.start, self.n = eng, sem, start, 0

    def __call__(self, instruction):
        instruction.then_inc(self.sem, 1)
        self.n += 1
        self.eng.wait_ge(self.sem, self.start + self.n)

    def all(self, *instructions):
        for instruction in instructions:
            instruction.then_inc(self.sem, 1)
        self.n += len(instructions)
        self.eng.wait_ge(self.sem, self.start + self.n)


class Core:

    def __init__(self, nc, ctx):
        self.nc, self.stage = nc, 0
        self.past = []
        self.tiles = 0
        self.outs = 0
        self.ahead = 0

        def sem(name):
            return ctx.enter_context(nc.semaphore(name))

        self.at = (nc.sbuf_base + 31) // 32 * 32
        sb = self.place
        self.const = sb("const", [P, C_KEPT])
        self.vec = sb("vec", [P, VEC_ROWS])
        self.small = sb("small", [P, 64])
        self.ring = sb("ring", [P, RING, 4, 512])
        self.wh = sb("wh", [P, 2, 4, 512], F32R)
        self.wl = sb("wl", [P, 2, 4, 512], F32R)
        self.x = sb("x", [P, NH, D])
        self.th = sb("th", [P, DC, T], F32R)
        self.tl = sb("tl", [P, DC, T], F32R)
        self.ps = ctx.enter_context(nc.psum_tensor("ps", [P, 8, 512], F32))
        self.landed = [sem(f"slab_landed{i}") for i in range(RING)]
        self.high_ready = sem("high_ready")
        self.low_ready = sem("low_ready")
        self.slabs_used = sem("slabs_used")
        self.outs_free = sem("outs_free")
        self.factor = self.small[:, 40:42]
        self.ident = self.const[:, C_ID:C_ID + P]
        self.arena = self.at

    def place(self, name, shape, dt=F32, at=None):
        at = self.at if at is None else self.arena + at
        size = 4 * int(np.prod(shape[1:]))
        self.at = at + (size + 31) // 32 * 32
        return self.nc.alloc_sbuf_tensor_at(name, shape, dt, offset=at)

    def scratch(self, at, *buffers):
        self.at = self.arena + at
        return [self.place(f"{b[0]}_{self.stage}", *b[1:]) for b in buffers]

    def v(self, name, chunk=0, n=1):
        return self.vec[:, VEC_AT[name] + chunk:VEC_AT[name] + chunk + n]

    def new(self, *names):
        self.stage += 1
        sems = [self.nc.alloc_semaphore(f"{n}_{self.stage}") for n in names]
        self.past += sems
        return sems

    def clear_semaphores(self):
        ids = sorted(int(s.num) for s in self.past)
        with self.nc.Block() as block:

            @block.gpsimd
            def _(pool):
                first = 0
                for n in range(1, len(ids) + 1):
                    if n == len(ids) or ids[n] != ids[n - 1] + 1:
                        pool.sem_clear(range(ids[first], ids[n - 1] + 1))
                        first = n

        for s in self.past:
            self.nc.release_semaphore(s)
        self.past = []


    def load_slab(self, sp, dma, tile, i, first=False):
        if not first:
            sp.wait_ge(self.low_ready, (tile - 1) * RING + (i + 1))
        src = dma(i)
        sp.dma_start(self.ring[:, i, :, 0:src.shape[-1]], src).then_inc(self.landed[i], 16)

    def split_high(self, act, tile, i, w=512):
        act.wait_ge(self.landed[i], tile * 16 + 16)
        act.wait_ge(self.slabs_used, tile * RING + (i + 1))
        self.nc.scalar.copy(self.wh[:, i % 2, :, 0:w], self.ring[:, i, :, 0:w]).then_inc(self.high_ready, 1)

    def split_low(self, dve, tile, i, w=512):
        dve.wait_ge(self.high_ready, tile * RING + (i + 1))
        self.nc.vector.tensor_tensor(self.wl[:, i % 2, :, 0:w], self.ring[:, i, :, 0:w],
                                     self.wh[:, i % 2, :, 0:w].bitcast(F32), ALU.subtract).then_inc(self.low_ready, 1)

    def multiply_slab(self, pe, tile, i, out, th, tl, chunk, start, stop, w=512):
        pe.wait_ge(self.low_ready, tile * RING + (i + 1))
        mm = self.nc.tensor.matmul
        for k in range(4):
            for half in range(NH):
                hi = th[:, chunk + k, half * P:(half + 1) * P]
                lo = tl[:, chunk + k, half * P:(half + 1) * P]
                wh, wl = self.wh[:, i % 2, k, 0:w], self.wl[:, i % 2, k, 0:w]
                o = self.ps[:, out + half, 0:w]
                mm(o, hi, wh, start=start and k == 0, stop=False)
                mm(o, hi, wl, start=False, stop=False)
                last = mm(o, lo, wh, start=False, stop=stop and k == 3)
        last.then_inc(self.slabs_used, 1)


def tile_view(w, col, width=512):
    rows = w.rearrange("(s c p) n -> s p c n", c=4, p=P)

    def slab(i):
        return rows[i, :, :, bass.ds(col, width)]

    return slab


def over_tiles(eng, n, body):
    body(0, 0)
    pairs = (n - 2) // 2
    if pairs > 1:
        with eng.Fori(0, pairs) as t:
            body(t * 2 + 1, 1)
            body(t * 2 + 2, 0)
    elif pairs == 1:
        body(1, 1)
        body(2, 0)
    for tile in range(2 * max(pairs, 0) + 1, n):
        body(tile, tile % 2)


def dense(core, name, n, source, evacuate, nexts, w=512, dve_slab=None, before=None,
          act_tile=None, dve_tile=None, act_slab=None, pool_part=None, after_tile=None):
    nc, base, outs = core.nc, core.tiles, core.outs
    split = core.ahead
    core.ahead = 1 if nexts is not None else 0
    next_w = nexts(0).shape[-1] if nexts is not None else 0

    def slabs(t):
        return range(split if isinstance(t, int) and t == 0 else 0, RING)

    def split_next(part, eng):
        if nexts is not None:
            part(eng, base + n, 0, next_w)

    with nc.Block() as block:

        @block.sync
        def _(sp):
            if before is not None:
                before(sp)
            if after_tile is not None:
                for t in range(1, n):
                    for i in range(RING):
                        core.load_slab(sp, source(t), t + base, i)
                    after_tile(sp, t)
            elif n > 1:
                with sp.Fori(1, n) as t:
                    for i in range(RING):
                        core.load_slab(sp, source(t), t + base, i)
            if nexts is not None:
                for i in range(RING):
                    core.load_slab(sp, nexts, base + n, i)

        @block.tensor
        def _(pe):
            def tile(t, parity):
                pe.wait_ge(core.outs_free, (t + outs) * 2 + 2)
                for i in range(RING):
                    core.multiply_slab(pe, t + base, i, 2 * parity, core.th, core.tl, 4 * i,
                                       i == 0, i == RING - 1, w)

            if n >= 4:
                with pe.Fori(0, n // 2) as t:
                    tile(t * 2, 0)
                    tile(t * 2 + 1, 1)
                if n % 2:
                    tile(n - 1, 0)
            else:
                for t in range(n):
                    tile(t, t % 2)

        @block.scalar
        def _(act):
            def read_out(t, parity):
                act.wait_ge(core.slabs_used, (t + base) * RING + (RING + 2))
                for half in range(NH):
                    evacuate(act, t, half, core.ps[:, 2 * parity + half, 0:w]).then_inc(core.outs_free, 1)

            def tile(t, parity):
                for i in range(RING):
                    if i in slabs(t):
                        core.split_high(act, t + base, i, w)
                    if i == 0 and not (isinstance(t, int) and t == 0):
                        read_out(t - 1, 1 - parity)

            if act_slab is None and act_tile is None:
                over_tiles(act, n, tile)
            else:
                for t in range(n):
                    for i in range(RING):
                        if i in slabs(t):
                            core.split_high(act, t + base, i, w)
                        if act_slab is not None:
                            if i == 0 and t:
                                read_out(t - 1, (t - 1) % 2)
                            act_slab(act, t * RING + i)
                        elif i == 1 and t:
                            act_tile(act, t - 1)
            split_next(core.split_high, act)
            if act_tile is None:
                read_out(n - 1, (n - 1) % 2)
            else:
                act_tile(act, n - 1)

        if pool_part is not None:

            @block.gpsimd
            def _(pool):
                pool_part(pool)

        @block.vector
        def _(dve):
            if dve_tile is not None or dve_slab is not None:
                for t in range(n):
                    for i in range(RING):
                        if i in slabs(t):
                            core.split_low(dve, t + base, i, w)
                        if dve_slab is not None:
                            dve_slab(dve, t * RING + i)
                        elif t and i in (0, 2):
                            dve_tile[i // 2](dve, t - 1)
            else:
                for i in slabs(0):
                    core.split_low(dve, base, i, w)
                if n > 1:
                    with dve.Fori(0, n - 1) as t:
                        for i in range(RING):
                            core.split_low(dve, t + (base + 1), i, w)
            split_next(core.split_low, dve)
            if dve_tile is not None:
                dve_tile[0](dve, n - 1)
                dve_tile[1](dve, n - 1)

    core.tiles += n
    core.outs += n


def transpose_split(core, src, chunks, hi, lo, sems, scale=None):
    nc = core.nc
    turned, high, low = sems

    def psum(c):
        return core.ps[:, 4 + c % 4, 0:T]

    def pe_part(pe, first=0, end=chunks):
        for c in range(first, end):
            if c >= 4:
                pe.wait_ge(low, c - 3)
            for half in range(NH):
                last = nc.tensor.transpose(psum(c)[:, half * P:(half + 1) * P],
                                           src[:, half, c * P:(c + 1) * P], core.ident)
            last.then_inc(turned, 1)

    def act_part(act, first=0, end=chunks):
        for c in range(first, end):
            act.wait_ge(turned, c + 1)
            kw = {} if scale is None else {"scale": scale(c)}
            nc.scalar.activation(hi[:, c, :], psum(c), ACT.Copy, **kw).then_inc(high, 1)

    def dve_part(dve):
        for c in range(chunks):
            dve.wait_ge(high, c + 1)
            h = hi[:, c, :].bitcast(F32)
            if scale is None:
                nc.vector.tensor_tensor(lo[:, c, :], psum(c), h, ALU.subtract).then_inc(low, 1)
            else:
                nc.vector.scalar_tensor_tensor(out=lo[:, c, :], in0=psum(c), scalar=scale(c), in1=h,
                                               op0=ALU.mult, op1=ALU.subtract).then_inc(low, 1)

    return pe_part, act_part, dve_part


def rms_factor(nc, dve, step, ms, out, tmp, width, eps, mean_ready, rooted, k):
    nc.vector.tensor_scalar(ms, ms, 1.0 / width, eps, ALU.mult, ALU.add).then_inc(mean_ready, 1)
    dve.wait_ge(rooted, k)
    step(nc.vector.reciprocal(out, tmp))
    step(nc.vector.tensor_tensor(tmp, out, out, ALU.mult))
    step(nc.vector.tensor_tensor(tmp, tmp, ms, ALU.mult))
    step(nc.vector.tensor_scalar(tmp, tmp, -0.5, 1.5, ALU.mult, ALU.add))
    step(nc.vector.tensor_tensor(out, out, tmp, ALU.mult))


def final_norm_stage(core, y, eps, buf, scratch, gain, out):
    nc, x = core.nc, core.x
    with ExitStack() as local:
        core.local = local
        done, sums, mean_ready, rooted, added, scaled, loaded, stored = core.new(
            "dve_done", "sums_ready", "mean_ready", "rooted", "x_ready", "normed", "gain_loaded", "stored")
        gains, = core.scratch(scratch, ("gain_rows", [P, D]))
        ms, rf, tmp = core.small[:, 0:2], core.small[:, 2:4], core.small[:, 4:6]
        rows = out.rearrange("(h p) d -> h p d", p=P)
        block = local.enter_context(nc.Block())

        @block.sync
        def _(sp):
            sp.dma_start(gains[:], gain.partition_broadcast(P)).then_inc(loaded, 16)
            for half in range(NH):
                sp.wait_ge(scaled, half + 1)
                sp.dma_start(rows[half], buf[:, half, :]).then_inc(stored, 16)
            sp.wait_ge(stored, 16 * NH)

        @block.scalar
        def _(act):
            for half in range(NH):
                act.wait_ge(added, half + 1)
                nc.scalar.activation(buf[:, half, :], x[:, half, :], ACT.Square,
                                     accum_out=ms[:, half:half + 1]).then_inc(sums, 1)
            act.wait_ge(mean_ready, 1)
            nc.scalar.activation(tmp, ms, ACT.Sqrt).then_inc(rooted, 1)

        @block.vector
        def _(dve):
            step = Steps(dve, done)
            for half in range(NH):
                nc.vector.tensor_tensor(x[:, half, :], x[:, half, :], y[:, half, :], ALU.add).then_inc(added, 1)
            dve.wait_ge(sums, 2)
            rms_factor(nc, dve, step, ms, rf, tmp, D, eps, mean_ready, rooted, 1)
            dve.wait_ge(loaded, 16)
            for half in range(NH):
                nc.vector.scalar_tensor_tensor(out=buf[:, half, :], in0=x[:, half, :], scalar=rf[:, half:half + 1],
                                               in1=gains[:], op0=ALU.mult, op1=ALU.mult).then_inc(scaled, 1)


def residual_stage(core, y, gain_name, eps, buf, scratch, post_gain=None, post_eps=None):
    nc, x = core.nc, core.x
    NQ, W = 4, D // 4
    with ExitStack() as local:
        core.local = local
        (done, y_sums, y_sums_dve, mean_ready, rooted, scaled, x_pool, x_dve, x_sums, turned, high,
         low) = core.new("dve_done", "y_sum_by_act", "y_sum_by_dve", "mean_ready", "rooted", "y_normed",
                            "x_by_pool", "x_by_dve", "x_sums", "turned", "high", "low")
        squares, junk = core.scratch(scratch, ("square_junk", [P, D]), ("junk_dve", [P, D]))
        ms, rf, tmp, parts = core.small[:, 0:2], core.small[:, 2:4], core.small[:, 4:6], core.small[:, 16:24]
        pe_part, act_part, dve_part = transpose_split(core, x, DC, core.th, core.tl, (turned, high, low),
                                                      lambda c: core.v(gain_name, c))
        quarter = [slice(q * W, (q + 1) * W) for q in range(NQ)]
        by_dve = NQ - 1
        term = y if post_gain is None else buf
        block = local.enter_context(nc.Block())

        def wait_x(eng, q):
            if y is not None:
                eng.wait_ge(*((x_dve, 1) if q == by_dve else (x_pool, q + 1)))

        @block.gpsimd
        def _(pool):
            if y is not None:
                for q in range(by_dve):
                    if post_gain is not None:
                        pool.wait_ge(scaled, 2 * q + 2)
                    nc.gpsimd.tensor_tensor(x[:, :, quarter[q]], x[:, :, quarter[q]], term[:, :, quarter[q]],
                                            ALU.add).then_inc(x_pool, 1)

        @block.scalar
        def _(act):
            if post_gain is not None:
                nc.scalar.activation(squares[:], y[:, 0, :], ACT.Square, accum_out=ms[:, 0:1]).then_inc(y_sums, 1)
                act.wait_ge(mean_ready, 1)
                nc.scalar.activation(tmp, ms, ACT.Sqrt).then_inc(rooted, 1)
            for q in range(NQ):
                act_part(act, 4 * q, 4 * q + 4)
                for half in range(NH):
                    wait_x(act, q)
                    n = NQ * half + q
                    nc.scalar.activation(squares[:, (n % 4) * W:(n % 4 + 1) * W], x[:, half, quarter[q]], ACT.Square,
                                         accum_out=parts[:, n:n + 1]).then_inc(x_sums, 1)
                    if half == 0:
                        act.wait_ge(x_sums, 2 * q + 1)
            act.wait_ge(mean_ready, 2 if post_gain is not None else 1)
            nc.scalar.activation(tmp, ms, ACT.Sqrt).then_inc(rooted, 1)

        @block.vector
        def _(dve):
            step = Steps(dve, done)
            if post_gain is not None:
                nc.vector.tensor_tensor_reduce(out=junk[:], in0=y[:, 1, :], in1=y[:, 1, :], scale=1.0, scalar=0.0,
                                               op0=ALU.mult, op1=ALU.add, accum_out=ms[:, 1:2]).then_inc(y_sums_dve, 1)
                dve.wait_ge(y_sums, 1)
                dve.wait_ge(y_sums_dve, 1)
                rms_factor(nc, dve, step, ms, rf, tmp, D, post_eps, mean_ready, rooted, 1)
                gains, loaded = post_gain
                dve.wait_ge(loaded, 16)
                for q in range(NQ):
                    for half in range(NH):
                        nc.vector.scalar_tensor_tensor(out=buf[:, half, quarter[q]], in0=y[:, half, quarter[q]],
                                                       scalar=rf[:, half:half + 1], in1=gains[:, quarter[q]],
                                                       op0=ALU.mult, op1=ALU.mult).then_inc(scaled, 1)
                dve.wait_ge(scaled, 2 * NQ)
            if y is not None:
                q = quarter[by_dve]
                nc.vector.tensor_tensor(x[:, :, q], x[:, :, q], term[:, :, q], ALU.add).then_inc(x_dve, 1)
            dve_part(dve)
            dve.wait_ge(x_sums, 2 * NQ)
            step(nc.vector.tensor_reduce(ms, parts.rearrange("p (h q) -> p h q", h=NH), AX.X, ALU.add))
            rms_factor(nc, dve, step, ms, core.factor, tmp, D, eps, mean_ready, rooted,
                       2 if post_gain is not None else 1)

        @block.tensor
        def _(pe):
            for q in range(NQ):
                wait_x(pe, q)
                pe_part(pe, 4 * q, 4 * q + 4)


def setup_stage(core, ins, first, turned_taps):
    nc = core.nc
    with ExitStack() as local:
        core.local = local
        const_in, rows_in, taps_in, x_in, turned, copied = core.new(
            "const_in", "rows_in", "taps_in", "x_in", "turned", "copied")
        rows, taps = core.scratch(0, ("vec_rows", [VEC_ROWS, P]), ("taps_rows", [TAPS, CW]))
        block = local.enter_context(nc.Block())

        @block.sync
        def _(sp):
            sp.dma_start(core.const[:], ins["shape_constants"][:, 0:C_KEPT]).then_inc(const_in, 16)
            sp.dma_start(core.x[:], ins["x"][0].rearrange("(h p) d -> p h d", p=P)).then_inc(x_in, 16)
            sp.wait_ge(x_in, 16)
            sp.wait_ge(rows_in, 16 * len(VECS))
            for i in range(RING):
                core.load_slab(sp, first, 0, i, first=True)

        @block.tensor
        def _(pe):
            pe.wait_ge(const_in, 16)
            pe.wait_ge(rows_in, 16 * len(VECS))
            nc.tensor.transpose(core.ps[:, 0, 0:VEC_ROWS], rows[:], core.ident[0:VEC_ROWS, 0:VEC_ROWS]).then_inc(turned, 1)
            pe.wait_ge(taps_in, 16)
            for c in range(CC):
                last = nc.tensor.transpose(core.ps[:, 1, c * 32:c * 32 + TAPS], taps[:, c * P:(c + 1) * P],
                                           core.ident[0:TAPS, 0:TAPS])
            last.then_inc(turned, 1)

        @block.scalar
        def _(act):
            for name, n in VECS:
                at = VEC_AT[name]
                src = ins[name][0]
                if len(src.shape) == 1:
                    src = src.rearrange("(c p) -> c p", p=P)
                act.dma_start(rows[at:at + n, :], src).then_inc(rows_in, 16)
            act.dma_start(taps[:], ins["w_dw"][0]).then_inc(taps_in, 16)

        @block.vector
        def _(dve):
            nc.vector.memset(core.small[:, 0:1], 0.0).then_inc(core.slabs_used, 2)
            nc.vector.memset(core.small[:, 1:2], 0.0).then_inc(core.outs_free, 4)
            dve.wait_ge(turned, 1)
            nc.vector.tensor_copy(core.vec[:], core.ps[:, 0, 0:VEC_ROWS]).then_inc(copied, 1)
            dve.wait_ge(turned, 2)
            nc.vector.tensor_copy(turned_taps[:, :, 0:TAPS],
                                  core.ps[:, 1, 0:CC * 32].rearrange("p (c k) -> p c k", k=32)[:, :, 0:TAPS]).then_inc(copied, 1)


def gated_stage(core, glu, ut):
    nc = core.nc
    with ExitStack() as local:
        core.local = local
        gates, gated, turned, read, pads = core.new("gates_ready", "gated", "turned", "read", "pads")
        block = local.enter_context(nc.Block())
        side = (TAPS - 1) // 2

        @block.scalar
        def _(act):
            for half in range(NH):
                nc.scalar.activation(glu[:, half, CW:], glu[:, half, CW:], ACT.Sigmoid).then_inc(gates, 1)
            for c in range(CC):
                act.wait_ge(turned, c + 1)
                nc.scalar.copy(ut[:, c, side:side + T], core.ps[:, 4 + c % 4, 0:T]).then_inc(read, 1)

        @block.vector
        def _(dve):
            for half in range(NH):
                dve.wait_ge(gates, half + 1)
                nc.vector.tensor_tensor(glu[:, half, :CW], glu[:, half, :CW], glu[:, half, CW:], ALU.mult).then_inc(gated, 1)

        @block.gpsimd
        def _(pool):
            nc.gpsimd.memset(ut[:, :, 0:side], 0.0).then_inc(pads, 1)
            nc.gpsimd.memset(ut[:, :, side + T:], 0.0).then_inc(pads, 1)

        @block.tensor
        def _(pe):
            pe.wait_ge(gated, NH)
            for c in range(CC):
                if c >= 4:
                    pe.wait_ge(read, c - 3)
                for half in range(NH):
                    last = nc.tensor.transpose(core.ps[:, 4 + c % 4, half * P:(half + 1) * P],
                                               glu[:, half, c * P:(c + 1) * P], core.ident)
                last.then_inc(turned, 1)


def conv_norm_stage(core, conv, xc, sq, stat, scratch):
    nc = core.nc
    flat = "p c t -> p (c t)"
    with ExitStack() as local:
        core.local = local
        ones_in, mean, centred, squared, var, var_in, rooted, normed, sig, act_out, high, low, done = core.new(
            "ones_in", "mean", "centred", "squared", "var", "var_in", "rooted", "normed", "sigmoid",
            "silu_ready", "high", "low", "dve_done")
        ones, = core.scratch(scratch, ("ones", [P, P]))
        block = local.enter_context(nc.Block())
        v_, r_, t_ = stat[:, 0, :], stat[:, 1, :], stat[:, 2, :]

        @block.gpsimd
        def _(pool):
            nc.gpsimd.memset(ones[:], 1.0 / CW).then_inc(ones_in, 1)

        @block.tensor
        def _(pe):
            pe.wait_ge(ones_in, 1)
            for c in range(CC):
                last = nc.tensor.matmul(core.ps[:, 4, 0:T], ones[:], conv[:, c, :], start=c == 0, stop=c == CC - 1)
            last.then_inc(mean, 1)
            for c in range(CC):
                pe.wait_ge(squared, c + 1)
                last = nc.tensor.matmul(core.ps[:, 5, 0:T], ones[:], sq[:, c, :], start=c == 0, stop=c == CC - 1)
            last.then_inc(var, 1)

        @block.scalar
        def _(act):
            for c in range(CC):
                act.wait_ge(centred, c + 1)
                nc.scalar.activation(sq[:, c, :], xc[:, c, :], ACT.Square).then_inc(squared, 1)
            act.wait_ge(var_in, 1)
            nc.scalar.activation(t_, v_, ACT.Sqrt).then_inc(rooted, 1)
            for c in range(CC):
                act.wait_ge(normed, c + 1)
                nc.scalar.activation(sq[:, c, :], xc[:, c, :], ACT.Sigmoid, scale=core.v("conv_ln_g", c),
                                     bias=core.v("conv_ln_b", c)).then_inc(sig, 1)
            for c in range(CC):
                act.wait_ge(act_out, c + 1)
                nc.scalar.copy(core.th[:, c, :], conv[:, c, :]).then_inc(high, 1)

        @block.vector
        def _(dve):
            step = Steps(dve, done)
            dve.wait_ge(mean, 1)
            for c in range(CC):
                nc.vector.tensor_tensor(xc[:, c, :], conv[:, c, :], core.ps[:, 4, 0:T], ALU.subtract).then_inc(centred, 1)
            dve.wait_ge(var, 1)
            nc.vector.tensor_scalar(v_, core.ps[:, 5, 0:T], 1e-5, None, ALU.add).then_inc(var_in, 1)
            dve.wait_ge(rooted, 1)
            step(nc.vector.reciprocal(r_, t_))
            step(nc.vector.tensor_tensor(t_, r_, r_, ALU.mult))
            step(nc.vector.tensor_tensor(t_, t_, v_, ALU.mult))
            step(nc.vector.tensor_scalar(t_, t_, -0.5, 1.5, ALU.mult, ALU.add))
            step(nc.vector.tensor_tensor(r_, r_, t_, ALU.mult))
            for c in range(CC):
                nc.vector.tensor_tensor(xc[:, c, :], xc[:, c, :], r_, ALU.mult).then_inc(normed, 1)
            for c in range(CC):
                dve.wait_ge(sig, c + 1)
                step(nc.vector.tensor_scalar(xc[:, c, :], xc[:, c, :], core.v("conv_ln_g", c),
                                             core.v("conv_ln_b", c), ALU.mult, ALU.add))
                nc.vector.tensor_tensor(conv[:, c, :], xc[:, c, :], sq[:, c, :], ALU.mult).then_inc(act_out, 1)
            for c in range(CC):
                dve.wait_ge(high, c + 1)
                nc.vector.tensor_tensor(core.tl[:, c, :], conv[:, c, :], core.th[:, c, :].bitcast(F32),
                                        ALU.subtract).then_inc(low, 1)


def turn_stage(core, src, chunks, out_for):
    nc = core.nc
    with ExitStack() as local:
        core.local = local
        turned, even_read, odd_read = core.new("turned", "even_read", "odd_read")
        block = local.enter_context(nc.Block())

        @block.tensor
        def _(pe):
            for c in range(chunks):
                if c >= 4:
                    pe.wait_ge(odd_read if c % 2 else even_read, c // 2 - 1)
                for half in range(NH):
                    last = nc.tensor.transpose(core.ps[:, 4 + c % 4, half * P:(half + 1) * P],
                                               src[:, half, c * P:(c + 1) * P], core.ident)
                last.then_inc(turned, 1)

        @block.scalar
        def _(act):
            for c in range(0, chunks, 2):
                act.wait_ge(turned, c + 1)
                nc.scalar.copy(out_for(c), core.ps[:, 4 + c % 4, 0:T]).then_inc(even_read, 1)

        @block.vector
        def _(dve):
            for c in range(1, chunks, 2):
                dve.wait_ge(turned, c + 1)
                nc.vector.tensor_copy(out_for(c), core.ps[:, 4 + c % 4, 0:T]).then_inc(odd_read, 1)


def attention_stage(core, heads, scale, spans, mask, products, v_of, vw, out, scratch, turn=None):
    nc = core.nc
    width = sum(n for _, n in spans)
    blocks = [(half, k) for half, (_, n) in enumerate(spans) for k in range(n // P)]
    with ExitStack() as local:
        core.local = local
        (laid, laid_act, laid_dve, scored, masked, peaked, exps, turned, copied, mixed, normed, summed) = core.new(
            "qk_turned", "qk_by_act", "qk_by_dve", "scores_ready", "masked", "max_ready", "probs_ready", "probs_turned", "probs_copied", "mixed", "normed", "inverted")
        s, p, pt, peak, total, inverse = core.scratch(
            scratch, ("scores_sb", [P, 2, width]), ("probs_sb", [P, 2, width]), ("probs_t", [P, 2, width]),
            ("peaks", [P, 2, 2]), ("totals", [P, heads, 2]), ("inverses", [P, heads, 2]))
        block = local.enter_context(nc.Block())
        lead = 1 if turn else 0
        rounds = range(heads + 2 + lead)

        @block.tensor
        def _(pe):
            for i in rounds:
                if turn and i < heads:
                    if i >= 1:
                        pe.wait_ge(laid_act, i)
                        pe.wait_ge(laid_dve, i)
                    for o, src in turn(i)[0]:
                        last = nc.tensor.transpose(o, src, core.ident)
                    last.then_inc(laid, 1)
                h = i - lead
                if 0 <= h < heads:
                    if turn:
                        pe.wait_ge(laid_act, h + 1)
                        pe.wait_ge(laid_dve, h + 1)
                    if h >= 2:
                        pe.wait_ge(masked, h - 1)
                    for half, (at, n) in enumerate(spans):
                        parts = products(h, half, n)
                        for j, (q, k) in enumerate(parts):
                            last = nc.tensor.matmul(core.ps[:, h % 2, at:at + n], q, k,
                                                    start=j == 0, stop=j == len(parts) - 1)
                    last.then_inc(scored, 1)
                h -= 1
                if 0 <= h < heads:
                    pe.wait_ge(exps, 2 * h + 2)
                    if h >= 2:
                        pe.wait_ge(copied, h - 1)
                    for half, k in blocks:
                        at = spans[half][0] + k * P
                        last = nc.tensor.transpose(core.ps[:, 2 + h % 2, at:at + P], p[:, h % 2, at:at + P], core.ident)
                    last.then_inc(turned, 1)
                h -= 1
                if 0 <= h < heads:
                    pe.wait_ge(copied, h + 1)
                    if h >= 2:
                        pe.wait_ge(normed, 2 * (h - 1))
                    for half, (at, n) in enumerate(spans):
                        for k in range(n // P):
                            last = nc.tensor.matmul(core.ps[:, 4 + h % 2, half * vw:(half + 1) * vw],
                                                    pt[:, h % 2, at + k * P:at + (k + 1) * P], v_of(h, k),
                                                    start=k == 0, stop=k == n // P - 1)
                    last.then_inc(mixed, 1)

        @block.scalar
        def _(act):
            for i in range(heads + lead):
                if turn and i < heads:
                    act.wait_ge(laid, i + 1)
                    if i >= 2:
                        act.wait_ge(scored, i - 1)
                    o, src = turn(i)[1]
                    nc.scalar.copy(o, src).then_inc(laid_act, 1)
                h = i - lead
                if 0 <= h < heads:
                    act.wait_ge(peaked, h + 1)
                    if h >= 2:
                        act.wait_ge(turned, h - 1)
                    for half, (at, n) in enumerate(spans):
                        nc.scalar.activation(p[:, h % 2, at:at + n], s[:, h % 2, at:at + n], ACT.Exp,
                                             bias=peak[:, h % 2, half:half + 1],
                                             accum_out=total[:, h, half:half + 1]).then_inc(exps, 1)

        @block.vector
        def _(dve):
            for i in rounds:
                if turn and i < heads:
                    dve.wait_ge(laid, i + 1)
                    if i >= 2:
                        dve.wait_ge(scored, i - 1)
                    o, src = turn(i)[2]
                    nc.vector.tensor_copy(o, src).then_inc(laid_dve, 1)
                h = i - lead
                if 0 <= h < heads:
                    dve.wait_ge(scored, h + 1)
                    if h >= 2:
                        dve.wait_ge(exps, 2 * (h - 1))
                    m = mask(h)
                    o, b = s[:, h % 2, :], core.ps[:, h % 2, 0:width]
                    if len(m.shape) == 3:
                        o, b = (z.rearrange("p (h k) -> p h k", h=m.shape[1]) for z in (o, b))
                    nc.vector.scalar_tensor_tensor(out=o, in0=b, scalar=scale, in1=m, op0=ALU.mult,
                                                   op1=ALU.add).then_inc(masked, 1)
                    dve.wait_ge(masked, h + 1)
                    for half, (at, n) in enumerate(spans):
                        last = nc.vector.tensor_reduce(peak[:, h % 2, half:half + 1], s[:, h % 2, at:at + n],
                                                       AX.X, ALU.max, negate=True)
                    last.then_inc(peaked, 1)
                h -= 1
                if 0 <= h < heads:
                    dve.wait_ge(turned, h + 1)
                    if h >= 2:
                        dve.wait_ge(mixed, h - 1)
                    nc.vector.tensor_copy(pt[:, h % 2, :], core.ps[:, 2 + h % 2, 0:width]).then_inc(copied, 1)
                    nc.vector.reciprocal(inverse[:, h, :], total[:, h, :]).then_inc(summed, 1)
                h -= 1
                if 0 <= h < heads:
                    dve.wait_ge(mixed, h + 1)
                    dve.wait_ge(summed, h + 1)
                    for half in range(NH):
                        nc.vector.tensor_scalar(out[:, half, h * vw:(h + 1) * vw],
                                                core.ps[:, 4 + h % 2, half * vw:(half + 1) * vw],
                                                inverse[:, h, half:half + 1], None, ALU.mult).then_inc(normed, 1)


def split_stage(core, src, chunks, hi, lo, scale=None):
    nc = core.nc
    with ExitStack() as local:
        core.local = local
        pe_part, act_part, dve_part = transpose_split(core, src, chunks, hi, lo,
                                                      core.new("turned", "high", "low"), scale)
        block = local.enter_context(nc.Block())
        block.tensor(pe_part)
        block.scalar(act_part)
        block.vector(dve_part)


def mlp_stage(core, w_up, w_down, total, nexts, scratch, before):
    nc, base, outs = core.nc, core.tiles, core.outs
    up_rows = w_up.rearrange("(s c p) n -> s p c n", c=4, p=P)
    down_rows = w_down.rearrange("(s c p) n -> s p c n", c=4, p=P)
    NT = D // 512
    split, core.ahead, next_w = core.ahead, 1, nexts(0).shape[-1]

    def up(q, n):
        return lambda i: up_rows[i, :, :, bass.ds(q * D + n * 512, 512)]

    def down(q, n):
        return lambda i: down_rows[q * 4 + i, :, :, n * 512:(n + 1) * 512]

    with ExitStack() as local:
        core.local = local
        cleared, squared, turned, f_high, f_low = core.new("cleared", "squared", "turned", "f_high", "f_low")
        fh, fl, relu, square = core.scratch(scratch, ("fh", [P, DC, T], F32R), ("fl", [P, DC, T], F32R),
                                            ("relu", [P, 2, NH, 512]), ("square", [P, 2, NH, 512]))
        block = local.enter_context(nc.Block())

        @block.sync
        def _(sp):
            before(sp)

            def quarter(q, last):
                for n in range(1, NT):
                    for i in range(RING):
                        core.load_slab(sp, up(q, n), q * (2 * NT) + (base + n), i)
                for n in range(NT):
                    for i in range(RING):
                        core.load_slab(sp, down(q, n), q * (2 * NT) + (base + NT + n), i)
                for i in range(RING):
                    core.load_slab(sp, nexts if last else up(q + 1, 0), q * (2 * NT) + (base + 2 * NT), i)

            with sp.Fori(0, QUARTERS - 1) as q:
                quarter(q, False)
            quarter(QUARTERS - 1, True)

        @block.tensor
        def _(pe):
            def turn(q, n):
                pe.wait_ge(squared, q * (2 * NT) + 2 * n + 2)
                pe.wait_ge(f_low, q * (2 * NT) + 2 * n + 2)
                for half in range(NH):
                    for j in range(4):
                        last = nc.tensor.transpose(core.ps[:, 4 + half, j * P:(j + 1) * P],
                                                   square[:, n % 2, half, j * P:(j + 1) * P], core.ident)
                    last.then_inc(turned, 1)

            with pe.Fori(0, QUARTERS) as q:
                for n in range(2 * NT):
                    tile = q * (2 * NT) + (base + n)
                    pe.wait_ge(core.outs_free, (q * (2 * NT) + (outs + n)) * 2 + 2)
                    for i in range(RING):
                        if n == NT:
                            pe.wait_ge(f_low, q * (2 * NT) + 2 * i + 4)
                        core.multiply_slab(pe, tile, i, 2 * (n % 2), *((core.th, core.tl) if n < NT else (fh, fl)),
                                           4 * i, i == 0, i == RING - 1)
                        if i == 1 and 1 <= n <= NT:
                            turn(q, n - 1)

        @block.scalar
        def _(act):
            def read_out(q, n):
                tile = q * (2 * NT) + (base + n)
                act.wait_ge(core.slabs_used, tile * RING + (RING + 2))
                for half in range(NH):
                    nc.scalar.activation(relu[:, n % 2, half, :], core.ps[:, 2 * (n % 2) + half, :],
                                         ACT.Relu, scale=core.factor[:, half:half + 1]).then_inc(core.outs_free, 1)

            def high(q, n):
                for half in range(NH):
                    act.wait_ge(turned, q * (2 * NT) + 2 * n + half + 1)
                    nc.scalar.copy(fh[:, 4 * n:4 * n + 4, half * P:(half + 1) * P],
                                   core.ps[:, 4 + half, :].rearrange("p (j t) -> p j t", j=4)).then_inc(f_high, 1)

            def quarter(q, split):
                for n in range(2 * NT):
                    for i in range(RING):
                        if n or i >= split:
                            core.split_high(act, q * (2 * NT) + (base + n), i)
                        if i == 0 and 1 <= n <= NT:
                            read_out(q, n - 1)
                        if i == 2 and 1 <= n <= NT:
                            high(q, n - 1)

            quarter(0, split)
            with act.Fori(0, QUARTERS - 1) as q:
                quarter(q + 1, 0)
            core.split_high(act, base + QUARTERS * 2 * NT, 0, next_w)

        @block.gpsimd
        def _(pool):
            nc.gpsimd.memset(total[:], 0.0).then_inc(cleared, 1)
            with pool.Fori(0, QUARTERS) as q:
                for n in range(NT):
                    pool.wait_ge(core.outs_free, (q * (2 * NT) + (outs + n)) * 2 + 6)
                    for half in range(NH):
                        r = relu[:, n % 2, half, :]
                        nc.gpsimd.tensor_tensor(square[:, n % 2, half, :], r, r, ALU.mult).then_inc(squared, 1)

        @block.vector
        def _(dve):
            nc.vector.memset(core.small[:, 62:63], 0.0).then_inc(f_low, 2)

            def read_out(q, n):
                tile = q * (2 * NT) + (base + NT + n)
                dve.wait_ge(core.slabs_used, tile * RING + (RING + 2))
                for half in range(NH):
                    o = total[:, half, n * 512:(n + 1) * 512]
                    nc.vector.tensor_tensor(o, core.ps[:, 2 * (n % 2) + half, :], o, ALU.add).then_inc(core.outs_free, 1)

            def low(q, n):
                for half in range(NH):
                    dve.wait_ge(f_high, q * (2 * NT) + 2 * n + half + 1)
                    o = (slice(None), slice(4 * n, 4 * n + 4), slice(half * P, (half + 1) * P))
                    nc.vector.tensor_tensor(fl[o], core.ps[:, 4 + half, :].rearrange("p (j t) -> p j t", j=4),
                                            fh[o].bitcast(F32), ALU.subtract).then_inc(f_low, 1)

            dve.wait_ge(cleared, 1)
            def first_tile(q, split, last_quarter=None):
                for i in range(split, RING):
                    core.split_low(dve, q * (2 * NT) + base, i)
                    if i == 0 and last_quarter is not None:
                        read_out(last_quarter, NT - 1)

            def others(q):
                for n in range(1, 2 * NT):
                    for i in range(RING):
                        core.split_low(dve, q * (2 * NT) + (base + n), i)
                        if i == 0 and n > NT:
                            read_out(q, n - 1 - NT)
                        if i == 2 and n <= NT:
                            low(q, n - 1)

            first_tile(0, split)
            with dve.Fori(0, QUARTERS - 1) as q:
                others(q)
                first_tile(q + 1, 0, q)
            others(QUARTERS - 1)
            core.split_low(dve, base + QUARTERS * 2 * NT, 0, next_w)
            read_out(QUARTERS - 1, NT - 1)
    core.tiles += QUARTERS * 2 * NT
    core.outs += QUARTERS * 2 * NT


def load_biases(sp, rpb, bias, biases_in, row):
    if row >= ROWS:
        return
    half, r = row // (P // GRID_W), row % (P // GRID_W)
    for k in range(ROWS):
        src = bass.AP(rpb.tensor, (WR - 1 + k - row) * (2 * WC - 1) + WC - GRID_W,
                      [[1, GRID_W], [(2 * WR - 1) * (2 * WC - 1), HEADS], [1, GRID_W]])
        dst = bias[r * GRID_W:(r + 1) * GRID_W, :, half, k * GRID_W:(k + 1) * GRID_W]
        sp.dma_start(dst, src).then_inc(biases_in, 16)


def rotate(nc, step, x1, x2, cos, sin, t1, t2):
    tt = nc.vector.tensor_tensor
    step(tt(t1, x1, sin, ALU.mult))
    step(tt(t2, x2, sin, ALU.mult))
    step(tt(x1, x1, cos, ALU.mult))
    step(tt(x2, x2, cos, ALU.mult))
    step(tt(x1, x1, t2, ALU.subtract))
    step(tt(x2, x2, t1, ALU.add))


def latent_stage(core, lat, ch, cl, kr, cos, sin, positions, scratch):
    nc = core.nc
    two_pi = 6.283185307179586
    c1 = 6.28125
    c2 = float(np.float32(two_pi - c1))
    c2 = float(np.float32(int(c2 * 2 ** 22) / 2 ** 22))
    c3 = float(np.float32(two_pi - c1 - c2))
    magic = 12582912.0
    with ExitStack() as local:
        core.local = local
        (pos_in, sums, mean_ready, rooted, done, scaled, turned, high, low, angles, tables, kr_ready, kr_turned,
         kr_read) = core.new(
            "pos_in", "sums_ready", "mean_ready", "rooted", "dve_done", "normed", "turned", "high", "low",
            "angles", "tables", "kr_ready", "kr_turned", "kr_read")
        junk, pos_i, pos, ang, turns, r_sin, r_cos, t1, t2 = core.scratch(
            scratch, ("junk", [P, 4, LORA]), ("pos_i", [P, NH], I32), ("pos", [P, NH]), ("ang", [P, NH, 32]),
            ("turns", [P, NH, 32]), ("r_sin", [P, NH, 32]), ("r_cos", [P, NH, 32]), ("t1", [P, NH, 32]),
            ("t2", [P, NH, 32]))
        ms, rf, tmp = core.small[:, 0:4], core.small[:, 4:8], core.small[:, 8:12]
        pe_part, act_part, dve_part = transpose_split(core, lat, 2 * LC, ch, cl, (turned, high, low),
                                                      lambda c: core.v("g_q_a_2", c))
        freq = core.const[:, C_FREQ:C_FREQ + 32]
        block = local.enter_context(nc.Block())

        @block.sync
        def _(sp):
            sp.dma_start(pos_i[:], positions.rearrange("b (h p) -> (b p) h", p=P),
                         allow_slow_non_contiguous=True).then_inc(pos_in, 16)

        @block.scalar
        def _(act):
            for j in range(4):
                nc.scalar.activation(junk[:, j, :], lat[:, j % 2, (j // 2) * LORA:(j // 2 + 1) * LORA], ACT.Square,
                                     accum_out=ms[:, j:j + 1]).then_inc(sums, 1)
            act.wait_ge(mean_ready, 1)
            nc.scalar.activation(tmp, ms, ACT.Sqrt).then_inc(rooted, 1)
            act_part(act)
            act.wait_ge(angles, 1)
            nc.scalar.activation(sin[:], r_sin[:], ACT.Sin).then_inc(tables, 1)
            nc.scalar.activation(cos[:], r_cos[:], ACT.Sin).then_inc(tables, 1)
            act.wait_ge(kr_turned, 1)
            nc.scalar.copy(kr[0:ROPE, :], core.ps[0:ROPE, 0, 0:T]).then_inc(kr_read, 1)

        @block.vector
        def _(dve):
            step = Steps(dve, done)
            dve.wait_ge(sums, 4)
            rms_factor(nc, dve, step, ms, rf, tmp, LORA, 1e-6, mean_ready, rooted, 1)
            for j in range(4):
                o = lat[:, j % 2, (j // 2) * LORA:(j // 2 + 1) * LORA]
                nc.vector.tensor_scalar(o, o, rf[:, j:j + 1], None, ALU.mult).then_inc(scaled, 1)
            dve_part(dve)
            dve.wait_ge(pos_in, 16)
            step(nc.vector.tensor_copy(pos[:], pos_i[:]))
            for half in range(NH):
                step(nc.vector.tensor_scalar(ang[:, half, :], freq, pos[:, half:half + 1], None, ALU.mult))
            for r, quarter in ((r_sin, 0.0), (r_cos, 0.25)):
                step(nc.vector.tensor_scalar(turns[:], ang[:], 1.0 / two_pi, quarter, ALU.mult, ALU.add))
                step(nc.vector.tensor_scalar(turns[:], turns[:], magic, None, ALU.add))
                step(nc.vector.tensor_scalar(turns[:], turns[:], magic, None, ALU.subtract))
                part = ang
                for c in (c1, c2, c3):
                    step(nc.vector.scalar_tensor_tensor(out=r[:], in0=turns[:], scalar=-c, in1=part[:],
                                                        op0=ALU.mult, op1=ALU.add))
                    part = r
                step(nc.vector.tensor_scalar(r[:], r[:], quarter * two_pi, None, ALU.add))
                ins = nc.vector.tensor_scalar(r[:], r[:], 3.1415925, -3.1415925, ALU.min, ALU.max)
                if quarter:
                    ins.then_inc(angles, 1)
                else:
                    step(ins)
            dve.wait_ge(tables, 2)
            k = lat[:, :, 2 * LORA:]
            rotate(nc, step, k[:, :, 0:32], k[:, :, 32:64], cos[:], sin[:], t1[:], t2[:])
            nc.vector.memset(core.small[:, 62:63], 0.0).then_inc(kr_ready, 1)

        @block.tensor
        def _(pe):
            pe.wait_ge(scaled, 4)
            pe_part(pe)
            pe.wait_ge(kr_ready, 1)
            for half in range(NH):
                last = nc.tensor.transpose(core.ps[0:ROPE, 0, half * P:(half + 1) * P],
                                           lat[:, half, 2 * LORA:], core.ident)
            last.then_inc(kr_turned, 1)


UQ_W = 384


def latent_sources(w_uq, w_ukv):
    uq = w_uq.rearrange("(c p) h k -> p c (h k)", p=P)
    ukv = w_ukv.rearrange("(c p) h k -> p c (h k)", p=P)

    def source(u):
        if u < 2:
            return lambda i: uq[:, :, (4 * u + i) * UQ_W:(4 * u + i + 1) * UQ_W]
        return lambda i: ukv[:, :, (4 * u + i - 8) * 512:(4 * u + i - 7) * 512]

    return source


def latent_dense(core, source, ch, cl, q, kv, nexts):
    nc, base, outs = core.nc, core.tiles, core.outs
    split, core.ahead = core.ahead, 1
    with nc.Block() as block:

        def width(s):
            return UQ_W if s < 8 else 512

        @block.sync
        def _(sp):
            for u in range(1, 4):
                for i in range(RING):
                    core.load_slab(sp, source(u), base + u, i)
            for i in range(RING):
                core.load_slab(sp, nexts, base + 4, i)

        @block.tensor
        def _(pe):
            for part in range(2):
                with pe.Fori(0, 2) as u:
                    for i in range(RING):
                        tile = u + (base + 2 * part)
                        pe.wait_ge(core.outs_free, u * 8 + (outs + 8 * part + i) * 2 + 2)
                        core.multiply_slab(pe, tile, i, 2 * (i % 2), ch, cl, LC * part, True, True, width(8 * part))

        @block.scalar
        def _(act):
            def read_out(s):
                act.wait_ge(core.slabs_used, base * RING + s + 3)
                w = width(s)
                o = q[:, :, s * w:(s + 1) * w] if s < 8 else kv[:, :, (s - 8) * w:(s - 7) * w]
                for half in range(NH):
                    nc.scalar.copy(o[:, half], core.ps[:, 2 * (s % 2) + half, 0:w]).then_inc(core.outs_free, 1)

            for s in range(16):
                if s >= split:
                    core.split_high(act, base + s // RING, s % RING, width(s))
                if s:
                    read_out(s - 1)
            core.split_high(act, base + 4, 0)
            read_out(15)

        @block.vector
        def _(dve):
            for s in range(split, 16):
                core.split_low(dve, base + s // RING, s % RING, width(s))
            core.split_low(dve, base + 4, 0)

    core.tiles += 4
    core.outs += 16


def rotate_stage(core, q, cos, sin, masks, scratch):
    nc = core.nc
    with ExitStack() as local:
        core.local = local
        done, made = core.new("dve_done", "masks_made")
        t1, t2 = core.scratch(scratch, ("t1", [P, HEADS, 32]), ("t2", [P, HEADS, 32]))
        block = local.enter_context(nc.Block())

        @block.gpsimd
        def _(pool):
            nc.gpsimd.memset(masks[:, P:2 * P], 0.0).then_inc(made, 1)
            for b in (0, 2):
                nc.gpsimd.tensor_copy(masks[:, b * P:(b + 1) * P], core.const[:, C_CAUSAL:C_CAUSAL + P]).then_inc(made, 1)

        @block.vector
        def _(dve):
            step = Steps(dve, done)
            for half in range(NH):
                heads = q[:, half, :].rearrange("p (h k) -> p h k", k=QK)
                c, s = (t[:, half, :].unsqueeze(1).broadcast_to([P, HEADS, 32]) for t in (cos, sin))
                rotate(nc, step, heads[:, :, NOPE:NOPE + 32], heads[:, :, NOPE + 32:], c, s, t1[:], t2[:])


def sgu_stage(core, z, w, g_rows, b_rows, w_in, g_in, b_in, scratch):
    nc = core.nc
    with ExitStack() as local:
        core.local = local
        (turned, w_ready, sums, sums_dve, centred, mean_ready, rooted, done, scaled, normed, mixed, read) = core.new(
            "turned", "w_ready", "sums_by_act", "sums_by_dve", "centred", "mean_ready", "rooted", "dve_done",
            "scaled", "normed", "mixed", "read")
        wt, junk = core.scratch(scratch, ("w_spatial_t", [P, GROUPS, P]), ("junk", [P, D]))
        mean, ms, rf, tmp = (core.small[:, k:k + 2] for k in (0, 2, 4, 6))
        tril = core.const[:, C_TRIL:C_TRIL + P]
        u, v = z[:, :, :D], z[:, :, D:]
        block = local.enter_context(nc.Block())

        def columns(g):
            return slice(g * GD, (g + 1) * GD)

        @block.tensor
        def _(pe):
            pe.wait_ge(w_in, 16)
            for g in range(GROUPS):
                last = nc.tensor.transpose(core.ps[:, g // 4, (g % 4) * P:(g % 4 + 1) * P], w[:, g, :], core.ident)
            last.then_inc(turned, 1)
            pe.wait_ge(w_ready, 2)
            for g in range(GROUPS):
                pe.wait_ge(normed, g + 1)
                if g >= 4:
                    pe.wait_ge(read, 2 * (g - 3))
                for half in range(NH):
                    last = nc.tensor.matmul(core.ps[:, 4 + g % 4, half * GD:(half + 1) * GD], wt[:, g, :],
                                            v[:, half, columns(g)], start=True, stop=True)
                last.then_inc(mixed, 1)

        @block.scalar
        def _(act):
            nc.scalar.activation(junk[:], v[:, 0, :], ACT.Identity, accum_out=mean[:, 0:1]).then_inc(sums, 1)
            act.wait_ge(sums, 1)
            act.wait_ge(centred, 1)
            nc.scalar.activation(junk[:], v[:, 0, :], ACT.Square, accum_out=ms[:, 0:1]).then_inc(sums, 1)
            act.wait_ge(sums, 2)
            act.wait_ge(centred, 2)
            nc.scalar.activation(junk[:], v[:, 1, :], ACT.Square, accum_out=ms[:, 1:2]).then_inc(sums, 1)
            act.wait_ge(mean_ready, 1)
            nc.scalar.activation(tmp, ms, ACT.Sqrt).then_inc(rooted, 1)

        @block.gpsimd
        def _(pool):
            pool.wait_ge(b_in, 16)
            for g in range(GROUPS):
                pool.wait_ge(scaled, 2 * g + 2)
                o = v[:, :, columns(g)]
                nc.gpsimd.tensor_tensor(o, o, b_rows[:, columns(g)].unsqueeze(1).broadcast_to([P, NH, GD]),
                                        ALU.add).then_inc(normed, 1)

        @block.vector
        def _(dve):
            step = Steps(dve, done)
            nc.vector.tensor_reduce(mean[:, 1:2], v[:, 1, :], AX.X, ALU.add).then_inc(sums_dve, 1)
            dve.wait_ge(sums, 1)
            dve.wait_ge(sums_dve, 1)
            step(nc.vector.tensor_scalar(mean, mean, 1.0 / D, None, ALU.mult))
            for half in range(NH):
                nc.vector.tensor_scalar(v[:, half, :], v[:, half, :], mean[:, half:half + 1], None,
                                        ALU.subtract).then_inc(centred, 1)
            dve.wait_ge(turned, 1)
            for b in range(2):
                nc.vector.tensor_tensor(wt[:, 4 * b:4 * b + 4, :], core.ps[:, b, :].rearrange("p (g t) -> p g t", g=4),
                                        tril.unsqueeze(1).broadcast_to([P, 4, P]), ALU.mult).then_inc(w_ready, 1)
            dve.wait_ge(sums, 3)
            rms_factor(nc, dve, step, ms, rf, tmp, D, 1e-6, mean_ready, rooted, 1)
            dve.wait_ge(g_in, 16)
            for g in range(GROUPS):
                for half in range(NH):
                    o = v[:, half, columns(g)]
                    nc.vector.scalar_tensor_tensor(out=o, in0=o, scalar=rf[:, half:half + 1], in1=g_rows[:, columns(g)],
                                                   op0=ALU.mult, op1=ALU.mult).then_inc(scaled, 1)
            for g in range(GROUPS):
                dve.wait_ge(mixed, g + 1)
                for half in range(NH):
                    o = u[:, half, columns(g)]
                    nc.vector.scalar_tensor_tensor(out=o, in0=core.ps[:, 4 + g % 4, half * GD:(half + 1) * GD],
                                                   scalar=core.v("b_spatial_2", g), in1=o, op0=ALU.add,
                                                   op1=ALU.mult).then_inc(read, 1)


def gates_stage(core, source, b_gate, oa, z, nexts, scratch):
    b_in, opened, scaled, merged = core.new("b_in", "opened", "scaled", "merged")
    rows, g = core.scratch(scratch, ("b_gate_rows", [P, 2 * D]), ("gates", [P, 2, NH, 512]))
    nc, base, outs = core.nc, core.tiles, core.outs
    n = 2 * D // 512

    def read_out(dve, t):
        if t == 0:
            dve.wait_ge(b_in, 16)
        if t >= 2:
            dve.wait_ge(*((scaled, t - 1) if t - 2 < n // 2 else (merged, t - 1 - n // 2)))
        dve.wait_ge(core.slabs_used, (t + base) * RING + (RING + 2))
        for half in range(NH):
            nc.vector.scalar_tensor_tensor(out=g[:, t % 2, half, :], in0=core.ps[:, 2 * (t % 2) + half, :],
                                           scalar=core.factor[:, half:half + 1], in1=rows[:, t * 512:(t + 1) * 512],
                                           op0=ALU.mult, op1=ALU.add).then_inc(core.outs_free, 1)

    def open_gates(act, t):
        act.wait_ge(core.outs_free, (t + outs) * 2 + 6)
        nc.scalar.activation(g[:, t % 2], g[:, t % 2], ACT.Sigmoid).then_inc(opened, 1)

    def merge(dve, t):
        dve.wait_ge(opened, t + 1)
        cols = slice(t % (n // 2) * 512, (t % (n // 2) + 1) * 512)
        if t < n // 2:
            nc.vector.tensor_tensor(oa[:, :, cols], oa[:, :, cols], g[:, t % 2], ALU.mult).then_inc(scaled, 1)
        else:
            nc.vector.tensor_tensor(g[:, t % 2], g[:, t % 2], z[:, :, cols], ALU.mult).then_inc(scaled, 1)
            dve.wait_ge(scaled, t + 1)
            nc.vector.tensor_tensor(oa[:, :, cols], oa[:, :, cols], g[:, t % 2], ALU.add).then_inc(merged, 1)

    dense(core, "gates", n, source, None, nexts,
          before=lambda sp: sp.dma_start(rows[:], b_gate.partition_broadcast(P)).then_inc(b_in, 16),
          act_tile=open_gates, dve_tile=(read_out, merge))


def key_stage(core, pq_t, keys, keys_t, keys_in, sub):
    nc = core.nc
    sets = 2 * PH
    with ExitStack() as local:
        core.local = local
        turned, copied, scored, read = core.new("turned", "copied", "scored", "read")
        block = local.enter_context(nc.Block())

        @block.tensor
        def _(pe):
            pe.wait_ge(keys_in, 16)
            for b in range(4):
                for j in range(4):
                    last = nc.tensor.transpose(core.ps[:, b, j * P:(j + 1) * P], keys[:, 4 * b + j, :], core.ident)
                last.then_inc(turned, 1)
            for half in range(NH):
                for b in range(4):
                    if half:
                        pe.wait_ge(read, b + 1)
                    else:
                        pe.wait_ge(copied, b + 1)
                    for j in range(4):
                        s = 4 * b + j
                        last = nc.tensor.matmul(core.ps[:, 4 + b, j * P:(j + 1) * P], pq_t[:, s, half * P:(half + 1) * P],
                                                keys_t[:, s, :], start=True, stop=True)
                    last.then_inc(scored, 1)

        @block.scalar
        def _(act):
            for b in range(4):
                act.wait_ge(turned, b + 1)
                nc.scalar.copy(keys_t[:, 4 * b:4 * b + 4, :], core.ps[:, b, :].rearrange("p (j n) -> p j n", j=4)).then_inc(copied, 1)

        @block.vector
        def _(dve):
            for n in range(8):
                half, b = n // 4, n % 4
                dve.wait_ge(scored, n + 1)
                nc.vector.tensor_copy(sub[:, half, 4 * b:4 * b + 4, :],
                                      core.ps[:, 4 + b, :].rearrange("p (j n) -> p j n", j=4)).then_inc(read, 1)


def pick_unit(core, dve, step, u, sub, b):
    nc, half, h = core.nc, u // PH, u % PH
    values = [sub[:, half, 2 * h + s, :] for s in range(2)]
    hot = core.const[:, C_IOTA:C_IOTA + TOPK].unsqueeze(1).broadcast_to([P, TOPK, TOPK])
    wide = [P, TOPK, TOPK]
    v = nc.vector

    step.all(*[v.max(b.best[:, s, 0:8], values[s]) for s in range(2)])
    step.all(*[v.max_index(b.best_at[:, s, 0:8], b.best[:, s, 0:8], values[s]) for s in range(2)],
             *[v.match_replace(b.rest[:, s, :], b.best[:, s, 0:8], values[s], -3e38) for s in range(2)])
    step.all(*[v.max(b.best[:, s, 8:16], b.rest[:, s, :]) for s in range(2)])
    cand = b.cand[:]
    step.all(*[v.max_index(b.best_at[:, s, 8:16], b.best[:, s, 8:16], b.rest[:, s, :]) for s in range(2)],
             v.tensor_tensor(cand.rearrange("p (a b) -> p a b", a=TOPK),
                             b.best[:, 0, :].unsqueeze(2).broadcast_to(wide),
                             b.best[:, 1, :].unsqueeze(1).broadcast_to(wide), ALU.add))
    top = b.top[:, u, :]
    step.all(v.tensor_copy(b.best_f[:], b.best_at[:]), v.max(top[:, 0:8], cand))
    step.all(v.max_index(b.top_at[:, 0:8], top[:, 0:8], cand),
             v.match_replace(b.cand_rest[:], top[:, 0:8], cand, -3e38))
    step.all(v.max(top[:, 8:16], b.cand_rest[:]))
    step.all(v.max_index(b.top_at[:, 8:16], top[:, 8:16], b.cand_rest[:]))
    step.all(v.tensor_scalar(b.place_u[:, 0, :], b.top_at[:], 4, None, ALU.logical_shift_right),
             v.tensor_scalar(b.place_u[:, 1, :], b.top_at[:], 15, None, ALU.bitwise_and))
    step.all(v.tensor_copy(b.place_f[:], b.place_u[:]))
    step.all(*[v.tensor_tensor(b.one_hot[:, s], hot, b.place_f[:, s, :].unsqueeze(2).broadcast_to(wide), ALU.is_equal)
               for s in range(2)])
    step.all(*[v.tensor_tensor(b.one_hot[:, s], b.one_hot[:, s], b.best_f[:, s, :].unsqueeze(1).broadcast_to(wide),
                               ALU.mult) for s in range(2)])
    where = slice(u * TOPK, (u + 1) * TOPK)
    step.all(*[v.tensor_reduce(b.keys_of[:, s, where], b.one_hot[:, s], AX.X, ALU.add) for s in range(2)])
    step.all(v.scalar_tensor_tensor(out=b.expert_f[:], in0=b.keys_of[:, 0, where], scalar=float(NKEYS),
                                    in1=b.keys_of[:, 1, where], op0=ALU.mult, op1=ALU.add))
    v.tensor_copy(b.index[:, where], b.expert_f[:]).then_inc(b.picked, 1)


class Named:
    pass


def expert_weights_stage(core, sub, h2, peer_u, first_v, counts, out, by_expert, scratch, kept):
    nc = core.nc
    UNITS = NH * PH
    with ExitStack() as local:
        core.local = local
        b = Named()
        (done, b.picked, primed, staged, freed, dots_kept, shifted, exped, gelued, weighted, turned, columns,
         rows_hot, rows_one, hot_used, distant, x_kept) = core.new(
            "dve_done", "unit_picked", "primed", "index_staged", "rows_used", "dots_kept", "shifted",
            "exponentiated", "gelued", "weighted", "picks_turned", "columns_copied", "rows_hot", "rows_one",
            "hot_used", "distant", "x_kept")
        cols_hot = core.new("cols_hot_low", "cols_hot_high")
        read, iota_in = core.new("spread_read", "iota_in")
        landed = core.new(*[f"row_landed{i}" for i in range(GR)])
        rows, = core.scratch(-112 * 1024, ("expert_rows", [P, GR, D]))
        (junk, b.best, b.best_at, b.rest, b.cand, b.cand_rest, b.best_f, b.top, b.top_at, b.place_u, b.place_f,
         b.one_hot, b.expert_f, b.index, total, slot, dot, carrier) = core.scratch(
            scratch, ("junk", [P, 2, D]), ("best", [P, 2, TOPK]), ("best_at", [P, 2, TOPK], U32),
            ("rest", [P, 2, NKEYS]), ("cand", [P, TOPK * TOPK]), ("cand_rest", [P, TOPK * TOPK]),
            ("best_f", [P, 2, TOPK]), ("top", [P, UNITS, TOPK]), ("top_at", [P, TOPK], U32),
            ("place_u", [P, 2, TOPK], U32), ("place_f", [P, 2, TOPK]), ("one_hot", [P, 2, TOPK, TOPK]),
            ("expert_f", [P, TOPK]), ("index", [P, NH * PICKS], U32), ("total", [P, PH]),
            ("index_slots", [P, GR], U32), ("dot_slots", [P, GR]), ("carrier", [P, 2]))
        b.keys_of, turned_keys, turned_weight, row_hot, col_hot = core.scratch(
            kept, ("keys_of", [P, 2, NH * PICKS]), ("turned_keys", [P, 2, P]), ("turned_weight", [P, P]),
            ("row_hot", [P, 8, NKEYS]), ("col_hot", [P, 8, NKEYS]))
        turned_w = turned_weight[:]
        iota = core.const[:, C_NA:C_NA + NKEYS]
        weight = core.const[:, C_NA + NKEYS:C_NA + NKEYS + NH * PICKS]
        block = local.enter_context(nc.Block())


        def rows_by_vector(dve, half, t, at):
            dve.wait_ge(hot_used, t + (half * P + at + 4))
            for i in range(4):
                n = at + i
                nc.vector.tensor_scalar(row_hot[:, n % 8, :], iota, turned_keys[:, 0, bass.ds(t + n, 1)],
                                        turned_w[:, bass.ds(t + n, 1)], ALU.is_equal, ALU.mult).then_inc(rows_hot, 1)

        def cols_by_vector(dve, half, t, at):
            dve.wait_ge(hot_used, t + (half * P + at + 4))
            nc.vector.tensor_tensor(col_hot[:, at % 8:at % 8 + 4, :], iota.unsqueeze(1).broadcast_to([P, 4, NKEYS]),
                                    turned_keys[:, 1, bass.ds(t + at, 4)].unsqueeze(2).broadcast_to([P, 4, NKEYS]),
                                    ALU.is_equal).then_inc(cols_hot[at % 8 // 4], 4)

        def hot_by_scalar(act, count, half, t, at, which):
            act.wait_ge(hot_used, t + (half * P + at + 4))
            for w in which:
                for i in range(4):
                    n = at + i
                    nc.scalar.activation((row_hot, col_hot)[w][:, n % 8, :], iota, ACT.Abs, scale=-1.0,
                                         bias=turned_keys[:, w, bass.ds(t + n, 1)]).then_inc(distant, 1)
            act.wait_ge(distant, count)
            for w in which:
                hot = (row_hot, col_hot)[w][:, at % 8:at % 8 + 4, :]
                nc.scalar.activation(hot, hot, ACT.Relu, scale=-1.0, bias=1.0).then_inc(
                    (rows_one, cols_hot[at % 8 // 4])[w], 4)

        def weigh_rows(pool, half, t, at):
            pool.wait_ge(rows_one, t + (half * P + at + 4))
            hot = row_hot[:, at % 8:at % 8 + 4, :]
            nc.gpsimd.tensor_tensor(hot, hot, turned_w[:, bass.ds(t + at, 4)].unsqueeze(2).broadcast_to([P, 4, NKEYS]),
                                    ALU.mult).then_inc(rows_hot, 4)

        @block.sync
        def _(sp):
            sp.dma_start(iota, counts).then_inc(iota_in, 16)
            sp.dma_start(out.rearrange("(h p) d -> p h d", p=P), core.x[:]).then_inc(x_kept, 16)
            sp.wait_ge(x_kept, 16)
            sp.wait_ge(freed, GR + UNITS * TOPK)
            for i in range(RING):
                core.load_slab(sp, first_v, core.tiles, i)

        @block.gpsimd
        def _(pool):
            nc.gpsimd.memset(carrier[:, 0:1], 0.0).then_inc(primed, 1)
            pool.wait_ge(primed, 1)

            def gather_unit(u, at, between=None):
                pool.wait_ge(b.picked, u + (at + 1))
                for j in range(TOPK):
                    i, n = j % GR, at * TOPK + j
                    pool.wait_ge(freed, u * TOPK + (n + 1))
                    nc.gpsimd.tensor_copy(slot[:, i:i + 1], b.index[:, bass.ds(u * TOPK + n, 1)]).then_inc(staged, 1)
                    pool.wait_ge(staged, u * TOPK + (n + 1))
                    nc.gpsimd.tensor_tensor(carrier[:, 1:2], carrier[:, 0:1], carrier[:, 0:1], ALU.mult)
                    nc.gpsimd.indirect_dma_start(
                        rows[:, i, :], None, peer_u, bass.IndirectOffsetOnAxis(ap=slot[:, i:i + 1], axis=0)
                    ).then_inc(landed[i], 16)
                    if between is not None and j % 4 == 3:
                        between(j - 3)

            with pool.Fori(0, PH) as u:
                gather_unit(u, 0)
            pool.wait_ge(iota_in, 16)
            with pool.Fori(0, PH) as u:
                gather_unit(u, PH, lambda at: weigh_rows(pool, 0, u * TOPK, at))

        @block.vector
        def _(dve):
            step = Steps(dve, done)
            nc.vector.memset(dot[:], 0.0).then_inc(freed, GR)
            nc.vector.memset(total[:], 0.0).then_inc(hot_used, 8)
            nc.vector.memset(b.best[:], 0.0).then_inc(read, 2)
            dve.wait_ge(read, 2)
            pick_unit(core, dve, step, 0, sub, b)
            for half in range(NH):
                for h in range(PH):
                    u = half * PH + h
                    if u + 1 < UNITS:
                        pick_unit(core, dve, step, u + 1, sub, b)
                    at = u * TOPK
                    with dve.Fori(0, TOPK // GR) as r:
                        for i in range(GR):
                            dve.wait_ge(landed[i], r * 16 + (at // GR * 16 + 16))
                            dve.wait_ge(freed, r * GR + (at + i + GR - 1))
                            nc.vector.tensor_tensor_reduce(out=junk[:, i % 2, :], in0=rows[:, i, :], in1=h2[:, half, :],
                                                           scale=1.0, scalar=0.0, op0=ALU.mult, op1=ALU.add,
                                                           accum_out=dot[:, i:i + 1]).then_inc(freed, 1)
                        dve.wait_ge(freed, r * GR + (at + 2 * GR))
                        nc.vector.tensor_copy(weight[:, bass.ds(r * GR + at, GR)], dot[:]).then_inc(dots_kept, 1)
                        dve.wait_ge(dots_kept, r + (at // GR + 1))
                mine = b.top[:, half * PH:(half + 1) * PH, :]
                wide = total[:].unsqueeze(2).broadcast_to([P, PH, TOPK])
                step(nc.vector.tensor_copy(total[:], b.top[:, half * PH:(half + 1) * PH, 0:1].rearrange("p g k -> p (g k)")))
                nc.vector.tensor_tensor(mine, mine, wide, ALU.subtract).then_inc(shifted, 1)
                dve.wait_ge(exped, half + 1)
                step(nc.vector.tensor_reduce(total[:], mine, AX.X, ALU.add))
                step(nc.vector.reciprocal(total[:], total[:]))
                step(nc.vector.tensor_tensor(mine, mine, wide, ALU.mult))
                w = weight[:, half * PICKS:(half + 1) * PICKS].rearrange("p (g k) -> p g k", k=TOPK)
                dve.wait_ge(gelued, half + 1)
                nc.vector.tensor_tensor(w, w, mine, ALU.mult).then_inc(weighted, 1)
            dve.wait_ge(iota_in, 16)
            dve.wait_ge(columns, 4)
            with dve.Fori(0, P // 8) as g:
                rows_by_vector(dve, 1, g * 8, 0)
                cols_by_vector(dve, 1, g * 8, 4)
                rows_by_vector(dve, 1, g * 8, 4)

        @block.tensor
        def _(pe):
            for half in range(NH):
                pe.wait_ge(weighted, half + 1)
                if half:
                    pe.wait_ge(columns, 2 * half)
                mine = slice(half * PICKS, (half + 1) * PICKS)
                for n, src in enumerate((b.keys_of[:, 0, mine], b.keys_of[:, 1, mine], weight[:, mine])):
                    last = nc.tensor.transpose(core.ps[:, 2, n * P:(n + 1) * P], src, core.ident)
                last.then_inc(turned, 1)
                with pe.Fori(0, P // 8) as g:
                    for i in range(8):
                        n = half * P + i
                        if i % 4 == 0:
                            pe.wait_ge(read, g * 2 + (n // 4 + 1))
                        pe.wait_ge(rows_hot, g * 8 + (n + 1))
                        pe.wait_ge(cols_hot[i // 4], g * 4 + (half * P // 2 + i % 4 + 1))
                        nc.tensor.matmul(core.ps[:, i // 4, i % 4 * P:(i % 4 + 1) * P], row_hot[:, i, :],
                                         col_hot[:, i, :], start=True, stop=True).then_inc(hot_used, 1)

        @block.scalar
        def _(act):
            for half in range(NH):
                act.wait_ge(dots_kept, (half + 1) * PICKS // GR)
                mine = weight[:, half * PICKS:(half + 1) * PICKS]
                nc.scalar.activation(mine, mine, ACT.Gelu_apprx_tanh).then_inc(gelued, 1)
                act.wait_ge(shifted, half + 1)
                mine = b.top[:, half * PH:(half + 1) * PH, :]
                nc.scalar.activation(mine, mine, ACT.Exp).then_inc(exped, 1)
                act.wait_ge(turned, half + 1)
                nc.scalar.copy(turned_keys[:], core.ps[:, 2, 0:2 * P].rearrange("p (s t) -> p s t", s=2)
                               ).then_inc(columns, 1)
                nc.scalar.copy(turned_w, core.ps[:, 2, 2 * P:3 * P]).then_inc(columns, 1)
                if half == 0:
                    act.wait_ge(x_kept, 16)
                act.wait_ge(iota_in, 16)
                act.wait_ge(columns, 2 * half + 2)
                which, fours = ((0, 1), (0, 4)) if half == 0 else ((1,), (0,))
                each = 4 * len(which)
                before = 2 * P * half

                def make(g, k, at):
                    hot_by_scalar(act, g * (each * len(fours)) + (before + each * (k + 1)), half, g * 8, at, which)

                def read_out(g, bank):
                    act.wait_ge(hot_used, g * 8 + (half * P + bank * 4 + 12))
                    nc.scalar.copy(by_expert[:, half, :, bass.ds(g * 8 + bank * 4, 4)],
                                   core.ps[:, bank, :].rearrange("p (t k) -> p k t", t=4)).then_inc(read, 1)

                for k, at in enumerate(fours):
                    make(0, k, at)
                with act.Fori(0, P // 8 - 1) as g:
                    for bank in range(2):
                        read_out(g, bank)
                        if bank < len(fours):
                            hot_by_scalar(act, g * (each * len(fours)) + (before + each * (len(fours) + bank + 1)),
                                          half, g * 8, 8 + fours[bank], which)
                for bank in range(2):
                    read_out(P // 8 - 1, bank)


def expert_source(peer_v):
    rows = peer_v.rearrange("(a g i) (c n) -> i a g c n", a=NKEYS, i=RING, c=4)

    def group(g):
        return lambda i: rows[i, :, bass.ds(g, 1), :, :].rearrange("a g c n -> a (g c) n")

    return group


def expert_sum_stage(core, by_expert, source, out, scratch):
    nc, base, groups = core.nc, core.tiles, NKEYS // RING
    with ExitStack() as local:
        core.local = local
        w_high, w_low, x_back = core.new("weights_high", "weights_low", "x_back")
        gh, gl = core.scratch(scratch, ("weights_high_part", [P, 2, NH, P], F32R),
                              ("weights_low_part", [P, 2, NH, P], F32R))
        block = local.enter_context(nc.Block())

        @block.sync
        def _(sp):
            with sp.Fori(1, groups) as g:
                for i in range(RING):
                    core.load_slab(sp, source(g), g + base, i)
            sp.wait_ge(core.slabs_used, (base + groups - 1) * RING + 2)
            sp.dma_start(core.x[:], out.rearrange("(h p) d -> p h d", p=P)).then_inc(x_back, 16)
            sp.wait_ge(x_back, 16)

        @block.scalar
        def _(act):
            with act.Fori(0, groups) as g:
                for i in range(RING):
                    act.wait_ge(core.slabs_used, (g + base) * RING + (i + 1))
                    nc.scalar.copy(gh[:, i % 2], by_expert[:, :, bass.ds(g * RING + i, 1), :].rearrange(
                        "p h k t -> p (h k) t")).then_inc(w_high, 1)
                    core.split_high(act, g + base, i)

        @block.vector
        def _(dve):
            with dve.Fori(0, groups) as g:
                for i in range(RING):
                    dve.wait_ge(w_high, g * RING + (i + 1))
                    nc.vector.tensor_tensor(gl[:, i % 2], by_expert[:, :, bass.ds(g * RING + i, 1), :].rearrange(
                        "p h k t -> p (h k) t"), gh[:, i % 2].bitcast(F32), ALU.subtract).then_inc(w_low, 1)
                    core.split_low(dve, g + base, i)

        @block.tensor
        def _(pe):
            mm = nc.tensor.matmul

            def slab(g, i, first, last):
                pe.wait_ge(w_low, g * RING + (i + 1))
                pe.wait_ge(core.low_ready, (g + base) * RING + (i + 1))
                wh, wl = core.wh[:, i % 2], core.wl[:, i % 2]
                for half in range(NH):
                    hi, lo = gh[:, i % 2, half, :], gl[:, i % 2, half, :]
                    for n, (weights, rows) in enumerate(((hi, wh), (hi, wl), (lo, wh))):
                        for k in range(4):
                            end = mm(core.ps[:, 4 * half + k, :], weights, rows[:, k, :],
                                     start=first and n == 0, stop=last and n == 2)
                end.then_inc(core.slabs_used, 1)

            for i in range(RING):
                slab(0, i, i == 0, False)
            with pe.Fori(1, groups - 1) as g:
                for i in range(RING):
                    slab(g, i, False, False)
            for i in range(RING):
                slab(groups - 1, i, False, i == RING - 1)

    core.tiles += groups


def build(nc, ins, out):
    with ExitStack() as ctx:
        core = Core(nc, ctx)
        KB = 1024
        place = core.place
        w_in, w_out, w_up, w_down = (ins[n][0] for n in ("w_in", "w_out", "w_up", "w_down"))
        w_in2, w_out2 = ins["w_in_2"][0], ins["w_out_2"][0]
        w_peer_q = ins["w_peer_q_2"][0].rearrange("d h k -> d (h k)")

        wdw_t = place("w_dw_turned", [P, CC, 32], at=34 * KB)
        setup_stage(core, ins, tile_view(w_in, 0), wdw_t)
        residual_stage(core, None, "pre_mix_g", 1e-6, None, 16 * KB)

        glu = place("a_and_gate", [P, NH, D], at=0)
        ut = place("gated_turned", [P, CC, PADT], at=16 * KB)
        conv = place("conv", [P, CC, T], at=26 * KB)
        qkv = place("qkv", [P, NH, 3 * CW], at=37152)
        bias = place("biases", [P, HEADS, NH, T], at=61728)

        def copy_to(dst):
            def evacuate(act, t, half, psum):
                return nc.scalar.copy(dst[:, half, bass.ds(t * 512, psum.shape[-1])], psum)
            return evacuate

        def scale_to(dst, func=ACT.Copy):
            def evacuate(act, t, half, psum):
                return nc.scalar.activation(dst[:, half, bass.ds(t * 512, psum.shape[-1])], psum, func,
                                            scale=core.factor[:, half:half + 1])
            return evacuate

        dense(core, "a_gate", 4, lambda t: tile_view(w_in, t * 512), scale_to(glu), tile_view(w_in, 2 * CW))
        gated_stage(core, glu, ut)
        with ExitStack() as local:
            core.local = local
            taps, biases_in, products, summed, masked_biases = core.new(
                "taps_done", "biases_in", "tap_products", "tap_products_summed", "biases_masked")
            SLOTS, SLABS = 8, 6 * RING
            product = place("tap_products", [P, SLOTS, T], at=6 * KB)
            work = [[(c, k) for c0 in pair for k in range(TAPS) for c in (c0, c0 + 1)] for pair in ((0, 2), (4, 6))]

            def share(slab, slabs):
                n = len(work[0])
                return range(min(slab * n // slabs, n), min((slab + 1) * n // slabs, n))

            def taps_by_vector(dve, slab):
                for n in share(slab, SLABS - 1):
                    c, k = work[0][n]
                    if k:
                        dve.wait_ge(taps, n - 1)
                    u, w = ut[:, c, k:k + T], wdw_t[:, c, k:k + 1]
                    if k == 0:
                        ins_ = nc.vector.tensor_scalar(conv[:, c, :], u, w, core.v("b_dw", c), ALU.mult, ALU.add)
                    else:
                        ins_ = nc.vector.scalar_tensor_tensor(out=conv[:, c, :], in0=u, scalar=w, in1=conv[:, c, :],
                                                              op0=ALU.mult, op1=ALU.add)
                    ins_.then_inc(taps, 1)

            def products_by_scalar(act, slab):
                for n in share(slab, SLABS - 6):
                    c, k = work[1][n]
                    if n >= SLOTS:
                        act.wait_ge(summed, n - SLOTS + 1)
                    bias_of = {"bias": core.v("b_dw", c)} if k == 0 else {}
                    nc.scalar.activation(product[:, n % SLOTS, :], ut[:, c, k:k + T], ACT.Identity,
                                         scale=wdw_t[:, c, k:k + 1], **bias_of).then_inc(products, 1)

            def sums_by_pool(pool):
                for n, (c, k) in enumerate(work[1]):
                    pool.wait_ge(products, n + 1)
                    if k == 0:
                        nc.gpsimd.tensor_copy(conv[:, c, :], product[:, n % SLOTS, :]).then_inc(summed, 1)
                    else:
                        pool.wait_ge(summed, n - 1)
                        nc.gpsimd.tensor_tensor(conv[:, c, :], conv[:, c, :], product[:, n % SLOTS, :],
                                                ALU.add).then_inc(summed, 1)
                pool.wait_ge(biases_in, 16 * ROWS * T // GRID_W)
                window = core.const[:, C_NA:C_NA + T].unsqueeze(1).broadcast_to([P, HEADS * NH, T])
                every = bias[:].rearrange("p h a t -> p (h a) t")
                nc.gpsimd.tensor_tensor(every, every, window, ALU.add).then_inc(masked_biases, 1)
                pool.wait_ge(masked_biases, 1)

            dense(core, "qkv", 6, lambda t: tile_view(w_in, t * 512 + 2 * CW), scale_to(qkv),
                  tile_view(w_out, 0), dve_slab=taps_by_vector, act_slab=products_by_scalar, pool_part=sums_by_pool,
                  after_tile=lambda sp, t: load_biases(sp, ins["rpb"][0], bias, biases_in, t - 1))

        xc = place("centred", [P, CC, T], at=0)
        sq = place("squares", [P, CC, T], at=8 * KB)
        stat = place("stats", [P, 3, T], at=16 * KB)
        conv_norm_stage(core, conv, xc, sq, stat, 19 * KB)

        q_t = place("q_turned", [P, CC, T], at=0)
        k_t = place("k_turned", [P, CC, T], at=8 * KB)
        attended = place("attended", [P, NH, CW], at=16 * KB)
        turn_stage(core, qkv, 2 * CC, lambda c: (q_t if c < CC else k_t)[:, c % CC, :])

        def na_products(h, half, n):
            at = (h % 2) * HD
            return [(q_t[at:at + HD, h // 2, half * P:(half + 1) * P], k_t[at:at + HD, h // 2, 0:n])]

        def head_biases(h):
            b = bias[:, h]
            return bass.AP(b.tensor, b.offset + GRID_W - 1, [list(b.ap[0]), [GRID_W, NH * ROWS], [-1, GRID_W]])

        attention_stage(core, HEADS, HD ** -0.5, ((0, T), (T, T)), head_biases, na_products,
                        lambda h, k: qkv[:, k, 2 * CW + h * HD:2 * CW + (h + 1) * HD], HD, attended, 24 * KB)
        split_stage(core, attended, CC, core.th[:, CC:, :], core.tl[:, CC:, :])

        mix = place("mix", [P, NH, D], at=0)
        normed = place("normed_2", [P, NH, D], at=16 * KB)
        mix_gain = place("post_mix_g_rows", [P, D], at=72 * KB)
        mlp_gain = place("post_mlp_g_rows", [P, D], at=64 * KB)
        mix_gain_in, mlp_gain_in = core.new("mix_gain_in", "mlp_gain_in")

        def load_rows(buf, vector, sem):
            return lambda sp: sp.dma_start(buf[:], vector.partition_broadcast(P)).then_inc(sem, 16)

        dense(core, "w_out", 4, lambda t: tile_view(w_out, t * 512), copy_to(mix), tile_view(w_up, 0),
              before=load_rows(mix_gain, ins["post_mix_g"][0], mix_gain_in))
        residual_stage(core, mix, "pre_mlp_g", 1e-6, normed, 32 * KB, post_gain=(mix_gain, mix_gain_in), post_eps=1e-6)

        mlp = place("mlp", [P, NH, D], at=48 * KB)
        mlp_stage(core, w_up, w_down, mlp, tile_view(w_in2, 2 * LORA, KPE_W), 0,
                  before=load_rows(mlp_gain, ins["post_mlp_g"][0], mlp_gain_in))
        normed = place("normed_3", [P, NH, D], at=0)
        residual_stage(core, mlp, "g_norm1_2", 1e-6, normed, 16 * KB, post_gain=(mlp_gain, mlp_gain_in), post_eps=1e-6)

        KPE, Z0 = 2 * LORA, 2 * LORA + ROPE
        lat = place("latents", [P, NH, 2 * LORA + ROPE], at=16 * KB)
        ch = place("latent_high", [P, 2 * LC, T], F32R, at=0)
        cl = place("latent_low", [P, 2 * LC, T], F32R, at=8 * KB)
        kr = place("rotated_key", [P, T], at=88 * KB)
        cos = place("cos", [P, NH, 32], at=89 * KB)
        sin = place("sin", [P, NH, 32], at=89 * KB + 256)
        source = latent_sources(ins["w_uq_2"][0], ins["w_ukv_2"][0])
        dense(core, "shared_key", 1, None, lambda act, t, half, psum: nc.scalar.activation(
            lat[:, half, KPE:], psum[:, 0:ROPE], ACT.Copy, scale=core.factor[:, half:half + 1]), tile_view(w_in2, 0), w=KPE_W)
        dense(core, "latents", 2, lambda t: tile_view(w_in2, t * 512), scale_to(lat), source(0))
        latent_stage(core, lat, ch, cl, kr, cos, sin, ins["positions_2"], 40 * KB)
        q = place("q", [P, NH, HEADS * QK], at=16 * KB)
        kv = place("kv", [P, NH, HEADS * 2 * NOPE], at=40 * KB)
        latent_dense(core, source, ch, cl, q, kv, tile_view(w_in2, Z0))
        causal3 = place("causal_masks", [P, 3 * P], at=90 * KB)
        rotate_stage(core, q, cos, sin, causal3, 72 * KB)

        oa = place("latent_attended", [P, NH, D], at=0)
        qk_t = place("head_qk_turned", [P, 2, 2 * T], at=72 * KB)
        qr_t = place("head_rotary_turned", [P, 2, T], at=76 * KB)

        def mla_turn(h):
            moves = []
            for half in range(NH):
                cols = slice(half * P, (half + 1) * P)
                moves.append((core.ps[:, 6, cols], q[:, half, h * QK:h * QK + NOPE]))
                moves.append((core.ps[:, 6, T + half * P:T + (half + 1) * P], kv[:, half, h * 2 * NOPE:(2 * h + 1) * NOPE]))
                moves.append((core.ps[0:ROPE, 7, cols], q[:, half, h * QK + NOPE:(h + 1) * QK]))
            return moves, (qk_t[:, h % 2, :], core.ps[:, 6, :]), (qr_t[0:ROPE, h % 2, :], core.ps[0:ROPE, 7, 0:T])

        def mla_products(h, half, n):
            cols = slice(half * P, (half + 1) * P)
            return [(qk_t[:, h % 2, cols], qk_t[:, h % 2, T:T + n]), (qr_t[0:ROPE, h % 2, cols], kr[0:ROPE, 0:n])]

        attention_stage(core, HEADS, QK ** -0.5, ((0, P), (P, T)), lambda h: causal3[:], mla_products,
                        lambda h, k: kv[:, k, (2 * h + 1) * NOPE:(2 * h + 2) * NOPE], VH, oa, 78 * KB, turn=mla_turn)

        core.clear_semaphores()
        z = place("z", [P, NH, 2 * D], at=16 * KB)

        w_spatial = place("w_spatial", [P, GROUPS, P], at=48 * KB)
        ln_g, ln_b = (place(f"sgu_ln_{n}_rows", [P, D], at=at * KB) for n, at in (("g", 52), ("b", 60)))
        sgu_in = core.new("w_spatial_in", "ln_g_in", "ln_b_in")

        def load_gating(sp):
            sp.dma_start(w_spatial[:], ins["w_spatial_2"][0].rearrange("g t s -> t g s")).then_inc(sgu_in[0], 16)
            sp.dma_start(ln_g[:], ins["sgu_ln_g_2"][0].partition_broadcast(P)).then_inc(sgu_in[1], 16)
            sp.dma_start(ln_b[:], ins["sgu_ln_b_2"][0].partition_broadcast(P)).then_inc(sgu_in[2], 16)

        dense(core, "z", 8, lambda t: tile_view(w_in2, t * 512 + Z0), scale_to(z, ACT.Gelu_apprx_tanh),
              tile_view(w_in2, Z0 + 2 * D), before=load_gating)
        sgu_stage(core, z, w_spatial, ln_g, ln_b, *sgu_in, 68 * KB)
        gates_stage(core, lambda t: tile_view(w_in2, t * 512 + (Z0 + 2 * D)), ins["b_gate_2"][0], oa, z,
                    tile_view(w_out2, 0), 48 * KB)
        split_stage(core, oa, DC, core.th, core.tl)
        y = place("merged_out", [P, NH, D], at=16 * KB)
        dense(core, "w_out_2", 4, lambda t: tile_view(w_out2, t * 512), copy_to(y), tile_view(w_peer_q, 0))

        h2 = place("h2", [P, NH, D], at=64 * KB)
        residual_stage(core, y, "g_norm2_2", 1e-6, None, 32 * KB)
        pq = place("peer_queries", [P, NH, D], at=0)
        gains = place("g_norm2_rows", [P, D], at=80 * KB)
        keys = place("keys", [P, 2 * PH, P], at=32 * KB)
        gains_in, keys_in, h2_ready = core.new("gains_in", "keys_in", "h2_ready")

        def norm_h2(dve, slab):
            if slab in (5, 9):
                half = slab // 9
                dve.wait_ge(gains_in, 16)
                nc.vector.scalar_tensor_tensor(out=h2[:, half, :], in0=core.x[:, half, :],
                                               scalar=core.factor[:, half:half + 1], in1=gains[:],
                                               op0=ALU.mult, op1=ALU.mult).then_inc(h2_ready, 1)

        def load_gains_and_keys(sp):
            sp.dma_start(gains[:], ins["g_norm2_2"][0].partition_broadcast(P)).then_inc(gains_in, 16)
            sp.dma_start(keys[:], ins["peer_keys_2"][0].rearrange("h s n k -> n (h s) k")).then_inc(keys_in, 16)

        dense(core, "w_peer_q", 4, lambda t: tile_view(w_peer_q, t * 512), scale_to(pq), None, dve_slab=norm_h2,
              before=load_gains_and_keys)
        pq_t = place("peer_queries_turned", [P, DC, T], at=16 * KB)
        turn_stage(core, pq, DC, lambda c: pq_t[:, c, :])
        keys_t = place("keys_turned", [P, 2 * PH, P], at=40 * KB)
        sub = place("key_scores", [P, NH, 2 * PH, NKEYS], at=48 * KB)
        key_stage(core, pq_t, keys, keys_t, keys_in, sub)
        by_expert = place("by_expert", [P, NH, NKEYS, P], at=-48 * KB)
        v_rows = expert_source(ins["peer_v_2"][0])
        expert_weights_stage(core, sub, h2, ins["peer_u_2"][0], v_rows(0),
                             ins["shape_constants"][:, C_IOTA:C_IOTA + NKEYS], out[0], by_expert, 16 * KB, 80 * KB)
        expert_sum_stage(core, by_expert, v_rows, out[0], 80 * KB)
        peer = core.ps[:].rearrange("p (h k) n -> p h (k n)", h=NH)
        last = place("result", [P, NH, D], at=0)
        final_norm_stage(core, peer, 1e-6, last, 16 * KB, ins["g_final_2"], out[0])


_INS = ["x", "w_in", "w_dw", "b_dw", "conv_ln_g", "conv_ln_b", "rpb", "w_out", "w_up", "w_down", "pre_mix_g",
        "post_mix_g", "pre_mlp_g", "post_mlp_g", "positions_2", "g_norm1_2", "w_in_2", "g_q_a_2", "w_uq_2",
        "g_kv_a_2", "w_ukv_2", "sgu_ln_g_2", "sgu_ln_b_2", "w_spatial_2", "b_spatial_2", "b_gate_2", "w_out_2",
        "g_norm2_2", "w_peer_q_2", "peer_keys_2", "peer_u_2", "peer_v_2", "g_final_2"]


def kernel(**inputs):
    import numpy as _np
    import concourse.bacc as _bacc
    from concourse import mybir as _mybir
    from concourse.bass_utils import run_bass_kernel_spmd as _run

    nc = _bacc.Bacc("TRN2", target_bir_lowering=False, num_devices=1)
    arrays, ins = {}, {}
    for name in _INS:
        a = _np.asarray(inputs[name])
        if name == "rpb":
            a = a[..., ::-1]
        a = _np.ascontiguousarray(a)
        arrays[f"in_{name}"] = a
        ins[name] = nc.dram_tensor(f"in_{name}", a.shape, _mybir.dt.from_np(a.dtype), kind="ExternalInput").ap()
    arrays["shape_constants"] = shape_constants()
    ins["shape_constants"] = nc.dram_tensor("shape_constants", (P, C_ALL), F32, kind="ExternalInput").ap()
    for name in ("peer_u_2", "peer_v_2"):
        assert ins[name].shape[0] == 1
    out = nc.dram_tensor("out", (1, T, D), F32, kind="ExternalOutput").ap()
    build(nc, ins, out)
    r = _run(nc, [arrays], core_ids=[0])
    return r.results[0]["out"]
```
